# Optimizing a Trainium2 kernel written in Bass

```python
import functools
import jax, jax.numpy as jnp
from jax import lax
import numpy as np

D_MODEL = 1024
BATCH = 1
SEQ = 1024
DEPTH = 1
DEC_BATCH = 8
DEC_SEQ = 16
PAST_LEN = 256

CHUNK = 64
Q_BLOCK = 128
SB_HEADS = 8
SB_HEAD_DIM = 64
SB_WIDTH = SB_HEADS * SB_HEAD_DIM
HG_HEADS = 4
HG_HEAD_DIM = 128
HG_WIDTH = HG_HEADS * HG_HEAD_DIM
MIX_WIDTH = SB_WIDTH + HG_WIDTH
IN_COLS = 3 * SB_WIDTH + 4 * HG_WIDTH
SPLITS = [SB_WIDTH, 2 * SB_WIDTH, 3 * SB_WIDTH, 3 * SB_WIDTH + HG_WIDTH,
          3 * SB_WIDTH + 2 * HG_WIDTH, 3 * SB_WIDTH + 3 * HG_WIDTH]
N_MEM = 256
MEM_HEADS = 4
MEM_HEAD_DIM = 128
MEM_WIDTH = MEM_HEADS * MEM_HEAD_DIM
D_FF = 4 * D_MODEL
EPS = 1e-6

kernel_name = 'hybrid_sb_hgrn2_stream_encoder'

def rmsnorm(x, gain):
    x32 = x.astype(jnp.float32)
    y = x32 * lax.rsqrt(jnp.mean(x32 * x32, axis=-1, keepdims=True) + EPS)
    return (y * gain.astype(jnp.float32)).astype(x.dtype)

def stick_breaking(q, k, v, q_pos, k_pos):
    z = jnp.einsum('bqhd,bkhd->bhqk', q.astype(jnp.float32), k.astype(jnp.float32)) * (SB_HEAD_DIM ** -0.5)
    mask = (k_pos[None, :] < q_pos[:, None])[None, None]
    log_keep = jnp.where(mask, -jax.nn.softplus(z), 0.0)
    rev = lax.cumsum(log_keep, axis=3, reverse=True)
    excl = jnp.concatenate([rev[..., 1:], jnp.zeros_like(rev[..., :1])], axis=-1)
    a = jnp.where(mask, jnp.exp(jax.nn.log_sigmoid(z) + excl), 0.0)
    return jnp.einsum('bhqk,bkhd->bqhd', a, v.astype(jnp.float32))

def sb_prompt(q, k, v):
    b, t, h, d = q.shape
    nb = t // Q_BLOCK
    pos = jnp.arange(t, dtype=jnp.int32)
    qb = q.reshape(b, nb, Q_BLOCK, h, d).transpose(1, 0, 2, 3, 4)
    pb = pos.reshape(nb, Q_BLOCK)
    out = lax.map(lambda a: stick_breaking(a[0], k, v, a[1], pos), (qb, pb))
    return out.transpose(1, 0, 2, 3, 4).reshape(b, t, h, d)

def sb_sample(past_k, past_v, q, k, v):
    p = past_k.shape[1]
    t = q.shape[1]
    k_all = jnp.concatenate([past_k.astype(k.dtype), k], axis=1)
    v_all = jnp.concatenate([past_v.astype(v.dtype), v], axis=1)
    q_pos = p + jnp.arange(t, dtype=jnp.int32)
    k_pos = jnp.arange(p + t, dtype=jnp.int32)
    return stick_breaking(q, k_all, v_all, q_pos, k_pos)

def hgrn2_chunked(q, k, v, log_f, s0):
    b, t, h, dk = q.shape
    dv = v.shape[-1]
    ln = min(CHUNK, t)
    nc = t // ln

    def to_chunks(a):
        return a.astype(jnp.float32).reshape(b, nc, ln, h, a.shape[-1]).transpose(1, 0, 2, 3, 4)

    tri = jnp.tril(jnp.ones((ln, ln), dtype=bool))[None, :, :, None, None]

    def step(s, inp):
        qc, kc, vc, gc = inp
        cum = jnp.cumsum(gc, axis=1)
        o_inter = jnp.einsum('blhk,bhkv->blhv', qc * jnp.exp(cum), s)
        diff = cum[:, :, None] - cum[:, None, :]
        decay = jnp.exp(jnp.where(tri, diff, -jnp.inf))
        scores = jnp.einsum('bthk,bshk,btshk->bths', qc, kc, decay)
        o_intra = jnp.einsum('bths,bshv->bthv', scores, vc)
        last = cum[:, -1]
        s_new = jnp.exp(last)[..., None] * s + jnp.einsum(
            'bshk,bshv->bhkv', kc * jnp.exp(last[:, None] - cum), vc)
        return s_new, o_inter + o_intra

    s_fin, o = lax.scan(step, s0.astype(jnp.float32),
                        (to_chunks(q), to_chunks(k), to_chunks(v), to_chunks(log_f)))
    o = o.transpose(1, 0, 2, 3, 4).reshape(b, t, h, dv)
    return o, s_fin

def memory_kv(mem, gain, w_mk, w_mv):
    b = mem.shape[0]
    h = rmsnorm(mem, gain)
    mk = (h @ w_mk).reshape(b, N_MEM, MEM_HEADS, MEM_HEAD_DIM)
    mv = (h @ w_mv).reshape(b, N_MEM, MEM_HEADS, MEM_HEAD_DIM)
    return mk, mv

def layer_forward(x, sb_fn, s0, mem_k, mem_v, lb, norm_mix, w_in, sb_gain, hg_gain, w_out,
                  norm_mem_q, w_mq, w_mo, norm_ffn, w_ffn1, w_ffn2):
    bx, t, _ = x.shape
    h = rmsnorm(x, norm_mix)
    proj = h @ w_in
    q_sb, k_sb, v_sb, q_hg, f_hg, i_hg, g_hg = jnp.split(proj, SPLITS, axis=-1)
    q_sb = q_sb.reshape(bx, t, SB_HEADS, SB_HEAD_DIM)
    k_sb = k_sb.reshape(bx, t, SB_HEADS, SB_HEAD_DIM)
    v_sb = v_sb.reshape(bx, t, SB_HEADS, SB_HEAD_DIM)
    o_sb = rmsnorm(sb_fn(q_sb, k_sb, v_sb).reshape(bx, t, SB_WIDTH), sb_gain)
    z = f_hg.astype(jnp.float32).reshape(bx, t, HG_HEADS, HG_HEAD_DIM)
    lb_h = lb.reshape(HG_HEADS, HG_HEAD_DIM)
    log_f = jnp.logaddexp(jnp.log(lb_h), jnp.log1p(-lb_h) + jax.nn.log_sigmoid(z))
    k_hg = (1.0 - lb_h) * jax.nn.sigmoid(-z)
    q_hg = q_hg.astype(jnp.float32).reshape(bx, t, HG_HEADS, HG_HEAD_DIM) * (HG_HEAD_DIM ** -0.5)
    i_hg = i_hg.reshape(bx, t, HG_HEADS, HG_HEAD_DIM)
    o_hg, s_new = hgrn2_chunked(q_hg, k_hg, i_hg, log_f, s0)
    gate = jax.nn.silu(g_hg.astype(jnp.float32).reshape(bx, t, HG_HEADS, HG_HEAD_DIM))
    o_hg = (rmsnorm(o_hg, hg_gain) * gate).reshape(bx, t, HG_WIDTH)
    mix = jnp.concatenate([o_sb.astype(x.dtype), o_hg.astype(x.dtype)], axis=-1)
    x = x + mix @ w_out
    h = rmsnorm(x, norm_mem_q)
    qm = (h @ w_mq).reshape(bx, t, MEM_HEADS, MEM_HEAD_DIM)
    sc = jnp.einsum('bqhd,bmhd->bhqm', qm.astype(jnp.float32), mem_k.astype(jnp.float32)) * (MEM_HEAD_DIM ** -0.5)
    p = jax.nn.softmax(sc, axis=-1)
    om = jnp.einsum('bhqm,bmhd->bqhd', p, mem_v.astype(jnp.float32)).reshape(bx, t, MEM_WIDTH)
    x = x + om.astype(x.dtype) @ w_mo
    h = rmsnorm(x, norm_ffn)
    x = x + jnp.square(jax.nn.relu(h @ w_ffn1)) @ w_ffn2
    return x, k_sb, v_sb, s_new

def setup_inputs(seed: int = 0) -> dict:
    key = jax.random.key(seed)
    ks = jax.random.split(key, 24)

    def nrm(k, shape, scale):
        return jax.random.normal(k, shape, jnp.float32) * scale

    def gain(k, shape):
        return 1.0 + 0.02 * jax.random.normal(k, shape, jnp.float32)

    return {
        'x_prompt': nrm(ks[0], (BATCH, SEQ, D_MODEL), 1.0),
        'x_sample': nrm(ks[1], (DEC_BATCH, DEC_SEQ, D_MODEL), 1.0),
        'mem_prompt': nrm(ks[2], (BATCH, N_MEM, D_MODEL), 1.0),
        'cache_sb_k': nrm(ks[3], (DEPTH, DEC_BATCH, PAST_LEN, SB_HEADS, SB_HEAD_DIM), 1.0),
        'cache_sb_v': nrm(ks[4], (DEPTH, DEC_BATCH, PAST_LEN, SB_HEADS, SB_HEAD_DIM), 1.0),
        'state_hgrn': nrm(ks[5], (DEPTH, DEC_BATCH, HG_HEADS, HG_HEAD_DIM, HG_HEAD_DIM), 0.3),
        'cache_mem_k': nrm(ks[6], (DEPTH, DEC_BATCH, N_MEM, MEM_HEADS, MEM_HEAD_DIM), 1.0),
        'cache_mem_v': nrm(ks[7], (DEPTH, DEC_BATCH, N_MEM, MEM_HEADS, MEM_HEAD_DIM), 1.0),
        'lb_logits': nrm(ks[8], (DEPTH, HG_WIDTH), 0.5),
        'norm_mix': gain(ks[9], (DEPTH, D_MODEL)),
        'w_in': nrm(ks[10], (DEPTH, D_MODEL, IN_COLS), D_MODEL ** -0.5),
        'sb_gain': gain(ks[11], (DEPTH, SB_WIDTH)),
        'hg_gain': gain(ks[12], (DEPTH, HG_HEADS, HG_HEAD_DIM)),
        'w_out': nrm(ks[13], (DEPTH, MIX_WIDTH, D_MODEL), MIX_WIDTH ** -0.5),
        'norm_mem_q': gain(ks[14], (DEPTH, D_MODEL)),
        'norm_mem_kv': gain(ks[15], (DEPTH, D_MODEL)),
        'w_mq': nrm(ks[16], (DEPTH, D_MODEL, MEM_WIDTH), D_MODEL ** -0.5),
        'w_mk': nrm(ks[17], (DEPTH, D_MODEL, MEM_WIDTH), D_MODEL ** -0.5),
        'w_mv': nrm(ks[18], (DEPTH, D_MODEL, MEM_WIDTH), D_MODEL ** -0.5),
        'w_mo': nrm(ks[19], (DEPTH, MEM_WIDTH, D_MODEL), MEM_WIDTH ** -0.5),
        'norm_ffn': gain(ks[20], (DEPTH, D_MODEL)),
        'w_ffn1': nrm(ks[21], (DEPTH, D_MODEL, D_FF), D_MODEL ** -0.5),
        'w_ffn2': nrm(ks[22], (DEPTH, D_FF, D_MODEL), D_FF ** -0.5),
        'norm_final': gain(ks[23], (D_MODEL,)),
    }

def reference(x_prompt, x_sample, mem_prompt, cache_sb_k, cache_sb_v, state_hgrn, cache_mem_k, cache_mem_v,
              lb_logits, norm_mix, w_in, sb_gain, hg_gain, w_out, norm_mem_q, norm_mem_kv, w_mq, w_mk, w_mv,
              w_mo, norm_ffn, w_ffn1, w_ffn2, norm_final):
    lb_all = jnp.cumsum(jax.nn.softmax(lb_logits.astype(jnp.float32), axis=0), axis=0)
    lb_all = lb_all - lb_all[:1]
    xp = x_prompt
    xs = x_sample
    kp_l, vp_l, sp_l, mkp_l, mvp_l, ks_l, vs_l, ss_l = [], [], [], [], [], [], [], []
    for l in range(DEPTH):
        shared = (lb_all[l], norm_mix[l], w_in[l], sb_gain[l], hg_gain[l], w_out[l],
                  norm_mem_q[l], w_mq[l], w_mo[l], norm_ffn[l], w_ffn1[l], w_ffn2[l])
        mk_p, mv_p = memory_kv(mem_prompt, norm_mem_kv[l], w_mk[l], w_mv[l])
        s0_p = jnp.zeros((xp.shape[0], HG_HEADS, HG_HEAD_DIM, HG_HEAD_DIM), jnp.float32)
        xp, kp, vp, sp = layer_forward(xp, sb_prompt, s0_p, mk_p, mv_p, *shared)
        xs, kn, vn, sn = layer_forward(xs, functools.partial(sb_sample, cache_sb_k[l], cache_sb_v[l]),
                                       state_hgrn[l], cache_mem_k[l], cache_mem_v[l], *shared)
        kp_l.append(kp); vp_l.append(vp); sp_l.append(sp); mkp_l.append(mk_p); mvp_l.append(mv_p)
        ks_l.append(kn); vs_l.append(vn); ss_l.append(sn)
    y_prompt = rmsnorm(xp, norm_final)
    y_sample = rmsnorm(xs, norm_final)
    return (y_prompt, y_sample, jnp.stack(kp_l), jnp.stack(vp_l), jnp.stack(sp_l), jnp.stack(mkp_l),
            jnp.stack(mvp_l), jnp.stack(ks_l), jnp.stack(vs_l), jnp.stack(ss_l))


_drawn_inputs = setup_inputs


def setup_inputs(seed=0):
    import zlib

    import numpy as np

    out = dict(_drawn_inputs(seed))
    spreads = {}
    factors = {'sb_gain': 4.648,
     'hg_gain': 8.0,
     'norm_mem_q': 8.0,
     'norm_mem_kv': 2.87,
     'norm_ffn': 3.711,
     'norm_final': 2.904}
    for name, (base, spread) in spreads.items():
        noise = np.random.default_rng([zlib.crc32(name.encode()), seed]).standard_normal(out[name].shape)
        drawn = base * np.exp(spread * noise) if base else spread * noise
        out[name] = __import__('jax').numpy.asarray(drawn.astype(out[name].dtype))
    for name, factor in factors.items():
        out[name] = (out[name] * factor).astype(out[name].dtype)
    return out
```

```python
from contextlib import ExitStack

import concourse.bass as bass
from concourse import mybir

F32 = mybir.dt.float32
F32R = mybir.dt.float32r
U8 = mybir.dt.uint8
ALU = mybir.AluOpType
ACT = mybir.ActivationFunctionType
AX_X = mybir.AxisListType.X

P = 128
D = 1024
KB = D // P
SEQ = 1024
NS, NQ = 8, 16
PAST = 256
NT = SEQ // P + 1
SMP = NT - 1
T = NT * P
TG = T // 3
SBW, HGW, MEMW = 512, 512, 512
HD = 64
PAIRS = SBW // P
HG_HEADS = HGW // P
NMEM = 256
MEM_HEADS = MEMW // P
DFF = 4 * D
FB = 4
FG = DFF // P // FB
EPS = 1e-6
CAP = 40.0
LEVELS = [1, 2, 4, 8, 16, 32, 64]
SLOTS = 4
RAWS = 2

C_ID, C_TRI, C_NEG, C_TRI16, C_NEG16, C_BLK, C_STR, C_ONE = 0, 128, 256, 384, 400, 416, 672, 680
C_END = 681


def shape_constants():
    import numpy as np

    p = np.arange(P)[:, None]
    f = np.arange(P)[None, :]
    j = np.arange(NQ)[None, :]
    cst = np.zeros((P, C_END), np.float32)
    cst[:, C_ID:C_ID + P] = p == f
    cst[:, C_TRI:C_TRI + P] = f < p
    cst[:, C_NEG:C_NEG + P] = np.where(f < p, 0.0, -1e30)
    cst[:, C_TRI16:C_TRI16 + NQ] = j < p % NQ
    cst[:, C_NEG16:C_NEG16 + NQ] = np.where(j < p % NQ, 0.0, -1e30)
    for g in range(2):
        own = np.arange(NS)[None, :] == g * 4 + p // 32
        cst[:, C_BLK + g * P:C_BLK + (g + 1) * P] = np.repeat(own, NQ, 1)
    cst[:, C_STR:C_STR + NS] = np.arange(NS)[None, :] == p // NQ
    cst[:, C_ONE] = 1.0
    lvl = np.zeros((P, len(LEVELS) + 1, P), np.float32)
    lvl[:, 0] = p == f
    for n, m in enumerate(LEVELS):
        lvl[:, n + 1] = (p // (2 * m) == f // (2 * m)) & (p % (2 * m) < m) & (f % (2 * m) >= m)
    keep = np.ones((P, T), np.float32)
    keep[:, 0:SEQ:P] = 0.0
    keep[:, SEQ::NQ] = 0.0
    return cst, lvl, keep


class Order:

    def __init__(self, eng, sem):
        self.eng, self.sem, self.n, self.it, self.per = eng, sem, 0, 0, 0

    def then(self, ins):
        ins.then_inc(self.sem, 1)
        self.n += 1
        self.eng.wait_ge(self.sem, self.it * self.per + self.n)

    def enter(self, it, per):
        self.it, self.per, self.start = it, per, self.n

    def leave(self, turns):
        assert self.n - self.start == self.per, (self.n - self.start, self.per)
        self.n += self.per * (turns - 1)
        self.it = self.per = 0


def build(nc, a, o, stop=99):
    ctx = ExitStack()
    with ctx:
        def sb(name, shape, dt=F32, where=ctx):
            return where.enter_context(nc.sbuf_tensor("sbuf_" + name, shape, dt))

        def sem(name):
            return ctx.enter_context(nc.semaphore(name))

        PS = ctx.enter_context(nc.psum_tensor("PS", [P, 8, 512], F32))
        cst = sb("cst", [P, C_END])
        lvl = sb("lvl", [P, len(LEVELS) + 1, P], U8)
        ident = cst[:, C_ID:C_ID + P]
        X = sb("X", [P, NT, D])
        h_hi = sb("h_hi", [P, KB, T], F32R)
        h_lo = sb("h_lo", [P, KB, T], F32R)
        raw = [sb(f"raw{i}", [P, 1024]) for i in range(RAWS)]
        w_hi = [sb(f"w_hi{i}", [P, 1024], F32R) for i in range(SLOTS)]
        w_lo = [sb(f"w_lo{i}", [P, 1024], F32R) for i in range(SLOTS)]

        half = sb("half", [P, NT])

        with ExitStack() as ph:
            s_qT = sb("s_qT", [P, T], where=ph)
            s_kT = sb("s_kT", [P, T], where=ph)
            s_k = sb("s_k", [P, NT, P], where=ph)
            s_v = sb("s_v", [P, NT, P], where=ph)
            s_E = sb("s_E", [P, 3, 1024], where=ph)
            s_aT = sb("s_aT", [P, 4, 512], where=ph)
            s_cK = sb("s_cK", [P, 8, P], where=ph)
            s_cV = sb("s_cV", [P, 8, P], where=ph)
            s_KT = sb("s_KT", [P, 4, PAST + NQ], where=ph)
            s_QB = sb("s_QB", [P, 640], where=ph)
            s_own = sb("s_own", [P, P], where=ph)
            s_oT = sb("s_oT", [P, P], where=ph)
        with ExitStack() as ph:
            g_qT = sb("g_qT", [P, T], where=ph)
            g_kT = sb("g_kT", [P, T], where=ph)
            g_cum = sb("g_cum", [P, T], where=ph)
            g_D = sb("g_D", [P, T], where=ph)
            g_QL = sb("g_QL", [P, T], where=ph)
            g_KL = sb("g_KL", [P, T], where=ph)
            g_I = sb("g_I", [P, NT, P], where=ph)
            g_G = sb("g_G", [P, NT, P], where=ph)
            g_A = sb("g_A", [P, NT, P], where=ph)
            g_S = sb("g_S", [P, NT - 1, P], where=ph)
            g_S0 = sb("g_S0", [P, NS, P], where=ph)
            g_keep = sb("g_keep", [P, T], where=ph)
            g_gain = sb("g_gain", [P, HGW], where=ph)
            g_word = sb("g_word", [P, 32], where=ph)
            g_el = sb("g_el", [P, 16], where=ph)
            g_st = sb("g_st", [P, 2, NT], where=ph)
        with ExitStack() as ph0:
            gain = sb("gain", [P, D], where=ph0)
            xn = sb("xn", [P, 2, D], where=ph0)
            st = sb("st", [P, 3, NT], where=ph0)
            with ExitStack() as ph:
                c_q = sb("c_q", [P, MEM_HEADS, T], where=ph)
                c_kT = sb("c_kT", [P, MEM_HEADS, NMEM], where=ph)
                c_v = sb("c_v", [P, 2, MEMW], where=ph)
                c_KT = sb("c_KT", [P, 4, NMEM], where=ph)
                c_V1 = sb("c_V1", [P, 8, P], where=ph)
                c_QB = sb("c_QB", [P, T], where=ph)
                c_P = sb("c_P", [P, 2, NMEM], where=ph)
                c_PT = sb("c_PT", [P, 2, NMEM], where=ph)
                c_st = sb("c_st", [P, 4, MEM_HEADS * NT], where=ph)
            with ExitStack() as ph:
                u_hi = sb("u_hi", [P, FB, T], F32R, where=ph)
                u_lo = sb("u_lo", [P, FB, T], F32R, where=ph)
                f_r = sb("f_r", [P, T], where=ph)
                f_s = xn[:].rearrange("p a b -> p (a b)")[:, 0:T]

        landed = [sem(f"landed{i}") for i in range(RAWS)]
        cut_hi = [sem(f"cut_hi{i}") for i in range(RAWS)]
        cut_lo = [sem(f"cut_lo{i}") for i in range(RAWS)]
        slot_free = [sem(f"slot_free{i}") for i in range(SLOTS)]

        def unit_sb(p, s):
            return p, (2 * p + s // 2 if s % 2 == 0 else p)

        def unit(c, s):
            return c + (PAIRS if s < 3 else 0), 2 * c + s // 2 + (2 * PAIRS if s % 2 == 0 else PAIRS)

        R_HG = 0
        R_OUT = HG_HEADS
        R_MEM = R_OUT + 2
        R_MQ = R_MEM + 2
        R_MO = R_MQ + 1
        R_FF = R_MO + 1

        def cut_hi_unit(act, use, s):
            k, n = use
            act.wait_ge(landed[s % 2], n * 16 + 16)
            act.wait_ge(slot_free[s], k + 1)
            act.activation(w_hi[s][:], raw[s % 2][:], ACT.Copy).then_inc(cut_hi[s % 2], 1)

        def cut_lo_unit(dve, use, s):
            k, n = use
            dve.wait_ge(landed[s % 2], n * 16 + 16)
            dve.wait_ge(slot_free[s], k + 1)
            dve.wait_ge(cut_hi[s % 2], n + 1)
            dve.tensor_tensor(w_lo[s][:], raw[s % 2][:], w_hi[s][:].bitcast(F32),
                              ALU.subtract).then_inc(cut_lo[s % 2], 1)

        def wait_unit(pe, use, s):
            k, n = use
            pe.wait_ge(cut_hi[s % 2], n + 1)
            pe.wait_ge(cut_lo[s % 2], n + 1)

        bar = sem("bar")
        ENGINES = 4

        def barrier(eng, n, joins=True):
            if joins:
                eng.drain().then_inc(bar, 1)
            eng.wait_ge(bar, ENGINES * n)

        def settle(eng):
            eng.wait_ge(ld("cst"), 32)

        io = {}

        def ld(name):
            if name not in io:
                io[name] = sem("ld_" + name)
            return io[name]

        N = {x: sem("norm_" + x) for x in ("sq", "ms", "rs", "xn", "tr", "hi", "lo", "out")}
        norm_tiles = [0]

        class Norm:
            def __init__(self, tag, tiles, width, src, at=0, final=False, loads=None, kbs=KB):
                self.tag, self.tiles, self.width, self.src, self.at, self.final = tag, tiles, width, src, at, final
                self.loads, self.kbs = loads, kbs
                self.base, norm_tiles[0] = norm_tiles[0], norm_tiles[0] + tiles

        def norm_act(act, n):
            def square(t):
                if n.loads:
                    act.wait_ge(n.loads[t], 16)
                if n.final:
                    if t >= 2:
                        act.wait_ge(N["out"], 16 * (t - 1))
                elif t >= 2:
                    act.wait_ge(N["tr"], 2 * (n.base + t - 1))
                if t >= 2:
                    act.wait_ge(N["xn"], n.base + t - 1)
                act.activation(xn[:, t % 2, 0:n.width], n.src(t)[:, 0:n.width], ACT.Square,
                               accum_out=st[:, 0, t:t + 1]).then_inc(N["sq"], 1)

            square(0)
            for t in range(n.tiles):
                if t + 1 < n.tiles:
                    square(t + 1)
                if not n.final:
                    for half_ in range(2):
                        act.wait_ge(N["tr"], 2 * (n.base + t) + half_ + 1)
                        act.activation(h_hi[:, 4 * half_:4 * half_ + 4, n.at + t * P:n.at + (t + 1) * P],
                                       PS[:, 2 * (t % 2) + half_, :].rearrange("p (k c) -> p k c", k=4),
                                       ACT.Copy).then_inc(N["hi"], 1)

        def norm_dve(dve, n):
            def scale(t):
                dve.wait_ge(N["sq"], n.base + t + 1)
                dve.tensor_scalar(st[:, 1, t:t + 1], st[:, 0, t:t + 1], 1.0 / n.width, EPS, ALU.mult, ALU.add)\
                   .then_inc(N["ms"], 1)

            def rows(t):
                dve.wait_ge(N["rs"], n.base + t + 1)
                dve.wait_ge(ld("gain"), 16 * n.gain_at)
                dve.scalar_tensor_tensor(xn[:, t % 2, 0:n.width], n.src(t)[:, 0:n.width], st[:, 2, t:t + 1],
                                         gain[:, 0:n.width], ALU.mult, ALU.mult).then_inc(N["xn"], 1)

            scale(0)
            rows(0)
            for t in range(n.tiles):
                if t + 1 < n.tiles:
                    scale(t + 1)
                    rows(t + 1)
                if not n.final:
                    for half_ in range(2):
                        dve.wait_ge(N["hi"], 2 * (n.base + t) + half_ + 1)
                        cols = slice(n.at + t * P, n.at + (t + 1) * P)
                        dve.tensor_tensor(h_lo[:, 4 * half_:4 * half_ + 4, cols],
                                          PS[:, 2 * (t % 2) + half_, :].rearrange("p (k c) -> p k c", k=4),
                                          h_hi[:, 4 * half_:4 * half_ + 4, cols].bitcast(F32),
                                          ALU.subtract).then_inc(N["lo"], 1)

        def norm_pool(pool, n):
            for t in range(n.tiles):
                pool.wait_ge(N["ms"], n.base + t + 1)
                pool.tensor_tensor(st[:, 2, t:t + 1], st[:, 1, t:t + 1], half[:, 0:1], ALU.pow)\
                    .then_inc(N["rs"], 1)

        def norm_pe(pe, n):
            for t in range(n.tiles):
                pe.wait_ge(N["xn"], n.base + t + 1)
                for half_ in range(2):
                    if t >= 2:
                        pe.wait_ge(N["lo"], 2 * (n.base + t - 2) + half_ + 1)
                    for k in range(4):
                        kb = 4 * half_ + k
                        src = xn[:, t % 2, kb * P:(kb + 1) * P] if kb * P < n.width else \
                            n.src(t)[:, kb * P:(kb + 1) * P]
                        last = pe.transpose(PS[:, 2 * (t % 2) + half_, k * P:(k + 1) * P], src, ident)
                    last.then_inc(N["tr"], 1)

        def project(pe, s, bank, ntok=T, group=TG):
            for g in range(ntok // group):
                tok = slice(g * group, (g + 1) * group)
                out = PS[:, bank + g, 0:group]
                for kb in range(KB):
                    hi, lo = w_hi[s][:, kb * P:(kb + 1) * P], w_lo[s][:, kb * P:(kb + 1) * P]
                    pe.matmul(out, hi, h_hi[:, kb, tok], start=kb == 0, stop=False)
                    pe.matmul(out, hi, h_lo[:, kb, tok], start=False, stop=False)
                    last = pe.matmul(out, lo, h_hi[:, kb, tok], start=False, stop=kb == KB - 1)
            last.then_inc(slot_free[s], 1)

        def projected(eng, use, s):
            eng.wait_ge(slot_free[s], use[0] + 2)

        def bank3(bank):
            return PS[:, bank:bank + 3, 0:TG]

        def as3(x):
            return x.rearrange("p (g c) -> p g c", g=3)

        sb_q, sb_kT, sb_vT = sem("sb_q"), sem("sb_kT"), sem("sb_vT")
        sb_tr = sem("sb_tr")
        sb_k, sb_v = sem("sb_k"), sem("sb_v")
        sb_st = sem("sb_st")
        sb_z = sem("sb_z")
        sb_min, sb_ex, sb_ln = sem("sb_min"), sem("sb_ex"), sem("sb_ln")
        sb_arg = sem("sb_arg")
        sb_a = sem("sb_a")
        sb_tc, sb_te = sem("sb_tc"), sem("sb_te")
        sb_av = sem("sb_av")
        sb_dv = sem("sb_dv")
        sb_prep = sem("sb_prep")
        sb_own = sem("sb_own")
        sb_so = sem("sb_so")
        sb_soT = sem("sb_soT")
        sb_x = sem("sb_x")
        sb_cK, sb_cV = sem("sb_cK"), sem("sb_cV")
        sb_cKf = sem("sb_cKf")

        U = 18
        chunks = []
        for u in range(16):
            i = u % 8
            chunks += [("a", u, c, min(4, i + 1 - c)) for c in range(0, i + 1, 4)]
            if u >= 14:
                chunks += [("K", u - 14, 0, 4), ("K", u - 14, 4, 4)]
        chunks += [("s", 16, 0, 3), ("s", 17, 0, 3)]
        NC = len(chunks)
        of_unit = {u: [c for c, x in enumerate(chunks) if x[0] in "as" and x[1] == u] for u in range(U)}
        of_K = {g: [c for c, x in enumerate(chunks) if x[0] == "K" and x[1] == g] for g in range(2)}
        av_index = {c: n for n, c in enumerate([c for c, x in enumerate(chunks) if x[0] in "as"])}
        NAV = len(av_index)

        def keys_of(u):
            return (u % 8 + 1) * P if u < 16 else PAST + NQ

        def zbanks(u):
            return PS[:, 2 * (u % 2):2 * (u % 2) + 2, :].rearrange("p b c -> p (b c)")[:, 0:keys_of(u)]

        def qb_blocks(x):
            return x.rearrange("p (s c) -> p s c", c=160)

        def sb_pe(pe):
            with pe.Fori(0, PAIRS) as p:
                for s in range(3):
                    wait_unit(pe, unit_sb(p, s), s)
                    if s == 2:
                        pe.wait_ge(sb_q, p + 1)
                    project(pe, s, 3 * (s % 2))
                for c in range(6):
                    if c == 0:
                        pe.wait_ge(sb_kT, p + 1)
                    if c == 3:
                        pe.wait_ge(sb_vT, p + 1)
                    if c in (2, 3, 4):
                        pe.wait_ge(sb_k, p * 3 + c - 1)
                    if c == 5:
                        pe.wait_ge(sb_v, p * 3 + 1)
                    src = s_kT[:, :] if c < 3 else s_E[:, 0:2, :].rearrange("p a b -> p (a b)")[:, 0:T]
                    for n, t in enumerate(range(4 * (c % 3), min(4 * (c % 3) + 4, NT))):
                        last = pe.transpose(PS[:, 6 + c % 2, n * P:(n + 1) * P], src[:, t * P:(t + 1) * P], ident)
                    last.then_inc(sb_tr, 1)

                def z(u):
                    if u >= 2:
                        pe.wait_ge(sb_arg, p * U + u - 1)
                    if u < 16:
                        rows = slice(HD * (u // 8), HD * (u // 8) + HD)
                        q = s_qT[rows, (u % 8) * P:(u % 8 + 1) * P]
                        for b in range((keys_of(u) + 511) // 512):
                            w = min(512, keys_of(u) - 512 * b)
                            last = pe.matmul(PS[:, 2 * (u % 2) + b, 0:w], q, s_kT[rows, 512 * b:512 * b + w],
                                             start=True, stop=True)
                    else:
                        for s in range(4):
                            last = pe.matmul(zbanks(u), s_QB[:, s * P:(s + 1) * P], s_KT[:, s, :],
                                             start=s == 0, stop=s == 3)
                    last.then_inc(sb_z, 1)

                def transposes(u):
                    pe.wait_ge(sb_a, p * U + u + 1)
                    for c in of_unit[u]:
                        _, _, first, n = chunks[c]
                        if c >= 2:
                            pe.wait_ge(sb_te, p * NC + c - 1)
                        for j in range(n):
                            if u >= 16 and j == 2:
                                pe.wait_ge(sb_own, p * 2 + u - 15)
                                src = s_own[:]
                            else:
                                src = s_E[:, u % 3, (first + j) * P:(first + j + 1) * P]
                            last = pe.transpose(PS[:, 4 + c % 2, j * P:(j + 1) * P], src, ident)
                        last.then_inc(sb_tc, 1)

                def cached_keys(g):
                    pe.wait_ge(sb_cK, p * 32 + 16 * g + 16)
                    for c in of_K[g]:
                        _, _, first, n = chunks[c]
                        pe.wait_ge(sb_te, p * NC + c - 1)
                        for j in range(n):
                            last = pe.transpose(PS[:, 4 + c % 2, j * P:(j + 1) * P], s_cK[:, first + j, :], ident)
                        last.then_inc(sb_tc, 1)
                    pe.wait_ge(sb_te, p * NC + of_K[g][-1] + 1)
                    pe.wait_ge(sb_prep, p * 2 + g + 1)

                def av(u):
                    for c in of_unit[u]:
                        _, _, first, n = chunks[c]
                        pe.wait_ge(sb_te, p * NC + c + 1)
                        w = s_aT[:, av_index[c] % 4, :]
                        if u < 16:
                            i, hh = u % 8, u // 8
                            for j in range(n):
                                kb = first + j
                                last = pe.matmul(PS[:, 6 + hh, i * HD:(i + 1) * HD], w[:, j * P:(j + 1) * P],
                                                 s_v[:, kb, hh * HD:(hh + 1) * HD], start=kb == 0, stop=kb == i)
                        else:
                            g = u - 16
                            if g == 0:
                                pe.wait_ge(sb_x, p * 3 + 1)
                            pe.wait_ge(sb_cV, p * 32 + 16 * g + 16)
                            o_ = PS[:, 6, g * P:(g + 1) * P]
                            pe.matmul(o_, s_v[:, SMP, :], w[:, 2 * P:3 * P], start=True, stop=False,
                                      skip_group_check=True)
                            for s in range(4):
                                for kt in range(2):
                                    last = pe.matmul(o_[:, s * 32:(s + 1) * 32], s_cV[:, 2 * s + kt, :],
                                                     w[:, kt * P + s * 32:kt * P + (s + 1) * 32],
                                                     start=False, stop=kt == 1, skip_group_check=True)
                        last.then_inc(sb_av, 1)

                pe.wait_ge(sb_v, p * 3 + 3)
                z(0)
                z(1)
                for u in range(U):
                    transposes(u)
                    if u == 14:
                        cached_keys(0)
                    if u == 15:
                        cached_keys(1)
                    if u + 2 < U:
                        z(u + 2)
                    av(u)
                pe.wait_ge(sb_so, p * 2 + 2)
                pe.transpose(PS[:, 4, 0:P], s_oT[:], ident).then_inc(sb_soT, 1)
                pe.wait_ge(sb_x, p * 3 + 3)

        def sb_act(act):
            with act.Fori(0, PAIRS) as p:
                projected(act, unit_sb(p, 0), 0)
                act.activation(as3(s_qT[:]), bank3(0), ACT.Copy, scale=HD ** -0.5).then_inc(sb_q, 1)
                projected(act, unit_sb(p, 2), 2)
                act.activation(as3(s_E[:, 0:2, :].rearrange("p a b -> p (a b)")[:, 0:T]), bank3(0), ACT.Copy)\
                   .then_inc(sb_vT, 1)
                for c in range(3, 6):
                    act.wait_ge(sb_tr, p * 6 + c + 1)
                    t0, t1 = 4 * (c - 3), min(4 * (c - 3) + 4, NT)
                    act.activation(s_v[:, t0:t1, :].rearrange("p t c -> p (t c)"), PS[:, 6 + c % 2, 0:(t1 - t0) * P],
                                   ACT.Copy).then_inc(sb_v, 1)

                def explog(u):
                    e = s_E[:, u % 3, 0:keys_of(u)]
                    act.wait_ge(sb_min, p * U + u + 1)
                    act.activation(e, e, ACT.Exp).then_inc(sb_ex, 1)
                    act.wait_ge(sb_ex, p * U + u + 1)
                    act.activation(e, e, ACT.Ln, bias=1.0).then_inc(sb_ln, 1)

                def weights(u):
                    e = s_E[:, u % 3, 0:keys_of(u)]
                    act.wait_ge(sb_arg, p * U + u + 1)
                    act.activation(e, e, ACT.Exp).then_inc(sb_a, 1)

                def copy_out(c):
                    kind, u, first, n = chunks[c]
                    act.wait_ge(sb_tc, p * NC + c + 1)
                    if kind == "K":
                        if u == 1 and first == 0:
                            act.wait_ge(sb_z, p * U + 17)
                        s0 = first // 2
                        act.activation(s_KT[:, s0:s0 + 2, 0:PAST],
                                       PS[:, 4 + c % 2, :].rearrange("p (s k) -> p s k", s=2),
                                       ACT.Copy).then_inc(sb_te, 1)
                    else:
                        if av_index[c] >= 4:
                            act.wait_ge(sb_av, p * NAV + av_index[c] - 3)
                        act.activation(s_aT[:, av_index[c] % 4, 0:n * P], PS[:, 4 + c % 2, 0:n * P], ACT.Copy)\
                           .then_inc(sb_te, 1)

                explog(0)
                for u in range(U):
                    if u + 1 < U:
                        explog(u + 1)
                    weights(u)
                    for c in of_unit[u]:
                        copy_out(c)
                    if u == 14:
                        for c in of_K[0]:
                            copy_out(c)
                    if u == 15:
                        for c in of_K[1]:
                            copy_out(c)
                    if u in (2, 4, 6):
                        s = u // 2 - 1
                        cut_hi_unit(act, unit_sb(p + 1, s), s)

        SB_DV = 78

        def sb_dve(dve):
            od = Order(dve, sb_dv)
            od.then(dve.memset(s_QB[:], 0.0))
            with dve.Fori(0, PAIRS) as p:
                od.enter(p, SB_DV)
                projected(dve, unit_sb(p, 1), 1)
                dve.tensor_copy(as3(s_kT[:]), bank3(3)).then_inc(sb_kT, 1)
                for c in range(3):
                    dve.wait_ge(sb_tr, p * 6 + c + 1)
                    t0, t1 = 4 * c, min(4 * c + 4, NT)
                    dve.tensor_copy(s_k[:, t0:t1, :].rearrange("p t c -> p (t c)"), PS[:, 6 + c % 2, 0:(t1 - t0) * P])\
                       .then_inc(sb_k, 1)

                def capped(u):
                    dve.wait_ge(sb_z, p * U + u + 1)
                    if u >= 3:
                        dve.wait_ge(sb_tc, p * NC + of_unit[u - 3][-1] + 1)
                    dve.tensor_scalar(s_E[:, u % 3, 0:keys_of(u)], zbanks(u), CAP, None, ALU.min)\
                       .then_inc(sb_min, 1)

                def exponent(u):
                    n = keys_of(u)
                    e = s_E[:, u % 3, 0:n]
                    w = P if u < 16 else NQ
                    tri, neg = (C_TRI, C_NEG) if u < 16 else (C_TRI16, C_NEG16)
                    dve.wait_ge(sb_ln, p * U + u + 1)
                    od.then(dve.tensor_tensor(e, e, zbanks(u), ALU.max))
                    od.then(dve.tensor_tensor(e[:, n - w:n], e[:, n - w:n], cst[:, tri:tri + w], ALU.mult))
                    od.then(dve.tensor_tensor_scan(e[:, ::-1], cst[:, C_ONE:C_ONE + 1].broadcast_to([P, n]),
                                                   e[:, ::-1], 0.0, ALU.mult, ALU.add))
                    od.then(dve.tensor_tensor(e, zbanks(u), e, ALU.subtract))
                    dve.tensor_tensor(e[:, n - w:n], e[:, n - w:n], cst[:, neg:neg + w], ALU.add)\
                       .then_inc(sb_arg, 1)

                def sample_group(g):
                    if g == 1:
                        dve.wait_ge(sb_z, p * U + 17)
                    for hh in range(2):
                        rows = slice(hh * HD, (hh + 1) * HD)
                        last = dve.tensor_copy(
                            qb_blocks(s_QB[rows, :])[:, :, hh * NQ:(hh + 1) * NQ],
                            s_qT[rows, SEQ + g * 64:SEQ + (g + 1) * 64].rearrange("p (s c) -> p s c", c=NQ))
                        od.then(last)
                    dve.tensor_copy(s_KT[:, :, PAST:PAST + NQ],
                                    s_kT[:, SEQ + g * 64:SEQ + (g + 1) * 64].rearrange("p (s c) -> p s c", c=NQ))\
                       .then_inc(sb_prep, 1)

                def own(g):
                    dve.wait_ge(sb_a, p * U + 17 + g)
                    if g == 1:
                        dve.wait_ge(sb_tc, p * NC + of_unit[16][-1] + 1)
                    dve.tensor_tensor(s_own[:].rearrange("p (s c) -> p s c", c=NQ),
                                      s_E[:, (16 + g) % 3, PAST:PAST + NQ].unsqueeze(1).broadcast_to([P, NS, NQ]),
                                      cst[:, C_BLK + g * P:C_BLK + (g + 1) * P].rearrange("p (s c) -> p s c", c=NQ),
                                      ALU.mult).then_inc(sb_own, 1)

                def head_out(hh):
                    dve.wait_ge(sb_av, p * NAV + 12 * (hh + 1))
                    dve.tensor_scalar(X[:, 0:SMP, bass.ds(p * P + hh * HD, HD)],
                                      PS[:, 6 + hh, :].rearrange("p (t c) -> p t c", c=HD), 1.0, None, ALU.mult)\
                       .then_inc(sb_x, 1)

                def sample_out(g):
                    dve.wait_ge(sb_av, p * NAV + 25 + g)
                    for hh in range(2):
                        rows = slice(hh * HD, (hh + 1) * HD)
                        ins = dve.tensor_copy(
                            s_oT[rows, g * 64:(g + 1) * 64].rearrange("p (s c) -> p s c", c=NQ),
                            PS[rows, 6, g * P:(g + 1) * P].rearrange("p (s c) -> p s c", c=32)
                            [:, :, hh * NQ:(hh + 1) * NQ])
                        if hh == 0:
                            od.then(ins)
                        else:
                            ins.then_inc(sb_so, 1)

                capped(0)
                for u in range(U):
                    if u + 1 < U:
                        capped(u + 1)
                    exponent(u)
                    if u == 8:
                        head_out(0)
                    if u in (14, 15):
                        sample_group(u - 14)
                    if u == 16:
                        head_out(1)
                        own(0)
                    if u == 17:
                        sample_out(0)
                        own(1)
                        sample_out(1)
                    if u in (2, 4, 6):
                        s = u // 2 - 1
                        cut_lo_unit(dve, unit_sb(p + 1, s), s)
                dve.wait_ge(sb_soT, p + 1)
                dve.tensor_scalar(X[:, SMP, bass.ds(p * P, P)], PS[:, 4, 0:P], 1.0, None, ALU.mult).then_inc(sb_x, 1)
                dve.wait_ge(sb_st, p * 64 + 64)
            od.leave(PAIRS)

        def tile_rows(x, cols):
            return x.rearrange("(t p) c -> p t c", p=P)[:, :, cols]

        names = ("q tcap tln lf karg k cum iT tr i gT g gcap gln gsp gsig gate darg dexp ql lvl pred "
                 "ecum qe kdarg kdexp kd kdt qem im u s o sout oh ms rs x st s0 dv el").split()
        G = {n: sem("hg_" + n) for n in names}
        lchunks = []
        for n in range(len(LEVELS) + 1):
            tiles = NT if n == 0 or LEVELS[n - 1] < NQ else SMP
            lchunks += [(n, t, min(4, tiles - t)) for t in range(0, tiles, 4)]
        NL = len(lchunks)
        NLV = len(LEVELS)

        def lcols(n):
            return T if n == 0 or LEVELS[n - 1] < NQ else SEQ

        def hg_pe(pe):
            with pe.Fori(0, HG_HEADS) as h:
                for s in range(4):
                    wait_unit(pe, unit(h, s), s)
                    if s == 2:
                        pe.wait_ge(G["q"], h + 1)
                    if s == 3:
                        pe.wait_ge(G["karg"], h + 1)
                    project(pe, s, 3 * (s % 2))
                for c in range(6):
                    if c == 0:
                        pe.wait_ge(G["iT"], h + 1)
                    if c == 3:
                        pe.wait_ge(G["gT"], h + 1)
                    if c in (2, 3, 4):
                        pe.wait_ge(G["i"], h * 3 + c - 1)
                    if c == 5:
                        pe.wait_ge(G["g"], h * 3 + 1)
                    src = g_QL if c < 3 else g_KL
                    for n, t in enumerate(range(4 * (c % 3), min(4 * (c % 3) + 4, NT))):
                        last = pe.transpose(PS[:, 6 + c % 2, n * P:(n + 1) * P], src[:, t * P:(t + 1) * P], ident)
                    last.then_inc(G["tr"], 1)
                pe.wait_ge(G["k"], h + 1)
                for c, (n, t0, nt) in enumerate(lchunks):
                    if t0 == 0 and n > 0:
                        pe.wait_ge(G["ql"], h * NLV + n)
                    if c >= 6:
                        pe.wait_ge(G["pred"], h * NL + c - 5)
                    ql, kl = (g_qT, g_kT) if n == 0 else (g_QL, g_KL)
                    for j in range(nt):
                        cols = slice((t0 + j) * P, (t0 + j + 1) * P)
                        last = pe.matmul(PS[:, c % 6, j * P:(j + 1) * P], kl[:, cols], ql[:, cols],
                                         start=True, stop=True)
                    last.then_inc(G["lvl"], 1)
                pe.wait_ge(G["kd"], h + 1)
                pe.wait_ge(G["g"], h * 3 + 3)
                for c in range(3):
                    if c == 2:
                        pe.wait_ge(G["kdt"], h * 3 + 1)
                    for n, t in enumerate(range(4 * c, min(4 * c + 4, NT))):
                        last = pe.transpose(PS[:, 6 + c % 2, n * P:(n + 1) * P], g_kT[:, t * P:(t + 1) * P], ident)
                    last.then_inc(G["tr"], 1)
                pe.wait_ge(G["kdt"], h * 3 + 3)
                pe.wait_ge(G["pred"], h * NL + NL)
                for t in range(SMP):
                    last = pe.matmul(PS[:, t // 4, (t % 4) * P:(t % 4 + 1) * P], g_QL[:, t * P:(t + 1) * P],
                                     g_I[:, t, :], start=True, stop=True)
                last.then_inc(G["u"], 1)
                pe.wait_ge(G["im"], h + 1)
                for b in range(2):
                    last = pe.matmul(PS[:, 2 + b, :], g_QL[:, SEQ:T], g_D[:, 512 * b:512 * (b + 1)],
                                     start=True, stop=True)
                last.then_inc(G["u"], 1)
                pe.wait_ge(G["qe"], h + 1)
                for t in range(SMP):
                    out = PS[:, 4 + t // 4, (t % 4) * P:(t % 4 + 1) * P]
                    last = pe.matmul(out, g_A[:, t, :], g_I[:, t, :], start=True, stop=t == 0)
                    if t > 0:
                        pe.wait_ge(G["s"], h * SMP + t)
                        last = pe.matmul(out, g_qT[:, t * P:(t + 1) * P], g_S[:, t - 1, :], start=False, stop=True)
                last.then_inc(G["o"], 1)
                pe.wait_ge(G["qem"], h + 1)
                pe.wait_ge(G["s0"], h * 16 + 16)
                out = PS[:, 6, 0:P]
                pe.matmul(out, g_A[:, SMP, :], g_I[:, SMP, :], start=True, stop=False)
                for s in range(NS):
                    last = pe.matmul(out, g_KL[:, s * P:(s + 1) * P], g_S0[:, s, :], start=False, stop=s == NS - 1)
                last.then_inc(G["o"], 1)
                pe.wait_ge(G["oh"], h * 2 + 2)
                pe.wait_ge(G["sout"], h + 1)

        def hg_act(act):
            def step(out, in_, f, s, **kw):
                act.activation(out, in_, f, **kw).then_inc(G[s], 1)

            with act.Fori(0, HG_HEADS) as h:
                projected(act, unit(h, 0), 0)
                step(as3(g_qT[:]), bank3(0), ACT.Copy, "q", scale=P ** -0.5)
                act.wait_ge(G["tcap"], h + 1)
                step(g_D[:], g_D[:], ACT.Exp, "tln", scale=-1.0)
                act.wait_ge(G["tln"], h * 2 + 1)
                step(g_D[:], g_D[:], ACT.Ln, "tln", bias=1.0)
                act.wait_ge(G["karg"], h + 1)
                step(g_kT[:], g_kT[:], ACT.Exp, "k")
                projected(act, unit(h, 2), 2)
                step(as3(g_QL[:]), bank3(0), ACT.Copy, "iT")
                for c in range(3):
                    act.wait_ge(G["tr"], h * 9 + c + 1)
                    t0, t1 = 4 * c, min(4 * c + 4, NT)
                    step(g_I[:, t0:t1, :].rearrange("p t c -> p (t c)"), PS[:, 6 + c % 2, 0:(t1 - t0) * P],
                         ACT.Copy, "i")
                act.wait_ge(G["gcap"], h + 1)
                step(g_D[:], g_D[:], ACT.Exp, "gln", scale=-1.0)
                act.wait_ge(G["gln"], h * 2 + 1)
                step(g_D[:], g_D[:], ACT.Ln, "gln", bias=1.0)
                act.wait_ge(G["gsp"], h + 1)
                step(g_D[:], g_D[:], ACT.Exp, "gsig", scale=-1.0)
                for n in range(1, NLV + 1):
                    act.wait_ge(G["darg"], h * NLV + n)
                    step(g_D[:, 0:lcols(n)], g_D[:, 0:lcols(n)], ACT.Exp, "dexp")
                    if n in (2, 3, 4, 5):
                        cut_hi_unit(act, unit(h + 1, n - 2), n - 2)
                act.wait_ge(G["ql"], h * NLV + NLV)
                step(g_D[:], g_cum[:], ACT.Exp, "ecum")
                act.wait_ge(G["kdarg"], h + 1)
                step(g_D[:], g_D[:], ACT.Exp, "kdexp")
                for c in range(3):
                    act.wait_ge(G["tr"], h * 9 + 7 + c)
                    t0, t1 = 4 * c, min(4 * c + 4, NT)
                    step(g_QL[:, t0 * P:t1 * P], PS[:, 6 + c % 2, 0:(t1 - t0) * P], ACT.Copy, "kdt")
                act.wait_ge(G["o"], h * 2 + 1)
                act.wait_ge(G["u"], h * 2 + 2)
                step(g_D[:, 0:SEQ].rearrange("p (b c) -> p b c", b=2), PS[:, 4:6, :], ACT.Copy, "oh")
                act.wait_ge(G["o"], h * 2 + 2)
                step(g_D[:, SEQ:T], PS[:, 6, 0:P], ACT.Copy, "oh")

        HG_DV = 6

        def hg_dve(dve):
            od = Order(dve, G["dv"])
            od.then(dve.memset(g_A[:], 0.0))

            def halves(x, n):
                m = LEVELS[n - 1]
                return x[:, 0:lcols(n)].rearrange("p (b h m) -> p b h m", h=2, m=m)

            with dve.Fori(0, HG_HEADS) as h:
                od.enter(h, HG_DV)
                z = bank3(3)
                projected(dve, unit(h, 1), 1)
                dve.tensor_scalar(as3(g_D[:]), z, -CAP, None, ALU.max).then_inc(G["tcap"], 1)
                dve.wait_ge(G["tln"], h * 2 + 2)
                od.then(dve.scalar_tensor_tensor(as3(g_cum[:]), as3(g_D[:]), -1.0, z, ALU.mult, ALU.min))
                dve.tensor_tensor(as3(g_kT[:]), as3(g_cum[:]), z, ALU.subtract).then_inc(G["karg"], 1)
                dve.wait_ge(ld("keep"), 16)
                dve.tensor_tensor_scan(g_cum[:], g_keep[:], g_cum[:], 0.0, ALU.mult, ALU.add).then_inc(G["cum"], 1)
                projected(dve, unit(h, 3), 3)
                dve.tensor_copy(as3(g_KL[:]), z).then_inc(G["gT"], 1)
                for c in range(3):
                    dve.wait_ge(G["tr"], h * 9 + c + 4)
                    t0, t1 = 4 * c, min(4 * c + 4, NT)
                    dve.tensor_copy(g_G[:, t0:t1, :].rearrange("p t c -> p (t c)"),
                                    PS[:, 6 + (c + 1) % 2, 0:(t1 - t0) * P]).then_inc(G["g"], 1)
                flatG = g_G[:].rearrange("p t c -> p (t c)")
                dve.wait_ge(G["g"], h * 3 + 3)
                dve.wait_ge(G["karg"], h + 1)
                dve.tensor_scalar(g_D[:], flatG, -CAP, None, ALU.max).then_inc(G["gcap"], 1)
                dve.wait_ge(G["gln"], h * 2 + 2)
                dve.scalar_tensor_tensor(g_D[:], flatG, -1.0, g_D[:], ALU.mult, ALU.max).then_inc(G["gsp"], 1)
                dve.wait_ge(G["gsig"], h + 1)
                dve.tensor_tensor(flatG, flatG, g_D[:], ALU.mult).then_inc(G["gate"], 1)
                dve.wait_ge(G["gate"], h + 1)
                dve.wait_ge(G["cum"], h + 1)

                def distance(n):
                    c, d = halves(g_cum[:], n), halves(g_D[:], n)
                    m = LEVELS[n - 1]
                    ref = c[:, :, 0, m - 1:m].broadcast_to([P, lcols(n) // (2 * m), m])
                    od_ = dve.tensor_tensor(d[:, :, 1, :], c[:, :, 1, :], ref, ALU.subtract)
                    dve.tensor_tensor(d[:, :, 0, :], ref, c[:, :, 0, :], ALU.subtract).then_inc(G["darg"], 1)

                def factors(n):
                    dve.wait_ge(G["dexp"], h * NLV + n)
                    if n > 1:
                        last = max(c for c, x in enumerate(lchunks) if x[0] == n - 1)
                        dve.wait_ge(G["lvl"], h * NL + last + 1)
                    d, q, k = (halves(x[:], n) for x in (g_D, g_qT, g_kT))
                    if n == 1:
                        dve.wait_ge(G["k"], h + 1)
                        dve.wait_ge(G["q"], h + 1)
                        dve.wait_ge(G["tr"], h * 9 + 6)
                    dve.tensor_tensor(halves(g_QL[:], n)[:, :, 1, :], q[:, :, 1, :], d[:, :, 1, :], ALU.mult)
                    dve.tensor_tensor(halves(g_KL[:], n)[:, :, 0, :], k[:, :, 0, :], d[:, :, 0, :], ALU.mult)\
                       .then_inc(G["ql"], 1)

                def pick(n):
                    for c, (lv, t0, nt) in enumerate(lchunks):
                        if lv != n:
                            continue
                        before = [b for b in range(c) if lchunks[b][1] == t0]
                        dve.wait_ge(G["lvl"], h * NL + c + 1)
                        if n > 0:
                            dve.wait_ge(G["pred"], h * NL + before[-1] + 1)
                        dve.memset(g_word[:, c:c + 1], 0.0)
                        dve.copy_predicated(g_A[:, t0:t0 + nt, :], lvl[:, n, :].unsqueeze(1).broadcast_to([P, nt, P]),
                                            PS[:, c % 6, 0:nt * P].rearrange("p (t c) -> p t c", c=P))\
                           .then_inc(G["pred"], 1)

                distance(1)
                factors(1)
                pick(0)
                for n in range(1, NLV + 1):
                    if n < NLV:
                        dve.wait_ge(G["ql"], h * NLV + n)
                        distance(n + 1)
                    pick(n)
                    if n < NLV:
                        factors(n + 1)
                    if n in (2, 3, 4, 5):
                        cut_lo_unit(dve, unit(h + 1, n - 2), n - 2)
                dve.wait_ge(G["ecum"], h + 1)
                dve.tensor_copy(g_el[:, 0:8], g_D[:, 0:SEQ].rearrange("p (t c) -> p t c", c=P)[:, :, P - 1])
                dve.tensor_copy(g_el[:, 8:16], g_D[:, SEQ:T].rearrange("p (t c) -> p t c", c=NQ)[:, :, NQ - 1])\
                   .then_inc(G["el"], 1)
                last = max(c for c in range(NL))
                dve.wait_ge(G["lvl"], h * NL + last + 1)
                dve.tensor_tensor(g_qT[:], g_qT[:], g_D[:], ALU.mult).then_inc(G["qe"], 1)
                dve.wait_ge(G["qe"], h + 1)
                dve.wait_ge(G["el"], h + 1)
                for lo, hi, c in ((0, SEQ, P), (SEQ, T, NQ)):
                    x = g_cum[:, lo:hi].rearrange("p (t c) -> p t c", c=c)
                    ins = dve.tensor_tensor(g_D[:, lo:hi].rearrange("p (t c) -> p t c", c=c),
                                            x[:, :, c - 1:c].broadcast_to([P, (hi - lo) // c, c]), x, ALU.subtract)
                ins.then_inc(G["kdarg"], 1)
                od.then(dve.memset(g_KL[:], 0.0))
                dve.tensor_copy(g_KL[:].rearrange("p (s c) -> p s c", c=P + NQ)[:, :, 0:NQ],
                                g_qT[:, SEQ:T].rearrange("p (s c) -> p s c", c=NQ)).then_inc(G["qem"], 1)
                dve.wait_ge(G["kdexp"], h + 1)
                dve.tensor_tensor(g_kT[:], g_kT[:], g_D[:], ALU.mult).then_inc(G["kd"], 1)
                dve.wait_ge(G["kd"], h + 1)
                dve.tensor_tensor(g_D[:, 0:SEQ].rearrange("p (s c) -> p s c", c=P),
                                  g_I[:, SMP, :].unsqueeze(1).broadcast_to([P, NS, P]),
                                  cst[:, C_STR:C_STR + NS].unsqueeze(2).broadcast_to([P, NS, P]),
                                  ALU.mult).then_inc(G["im"], 1)
                dve.wait_ge(G["u"], h * 2 + 1)
                for t in range(SMP):
                    u = PS[:, t // 4, (t % 4) * P:(t % 4 + 1) * P]
                    if t == 0:
                        ins = dve.tensor_copy(g_S[:, 0, :], u)
                    else:
                        dve.wait_ge(G["s"], h * SMP + t)
                        ins = dve.scalar_tensor_tensor(g_S[:, t, :], g_S[:, t - 1, :], g_el[:, t:t + 1], u,
                                                       ALU.mult, ALU.add)
                    ins.then_inc(G["s"], 1)
                dve.wait_ge(G["u"], h * 2 + 2)
                dve.wait_ge(G["o"], h * 2 + 2)
                for s in range(NS):
                    ins = dve.scalar_tensor_tensor(g_S0[:, s, :], g_S0[:, s, :], g_el[:, 8 + s:9 + s],
                                                   PS[:, 2 + s // 4, (s % 4) * P:(s % 4 + 1) * P],
                                                   ALU.mult, ALU.add)
                ins.then_inc(G["sout"], 1)
                dve.wait_ge(G["oh"], h * 2 + 2)
                od.then(dve.tensor_tensor(g_cum[:], g_D[:], g_D[:], ALU.mult))
                od.then(dve.tensor_reduce(g_st[:, 0, :], g_cum[:].rearrange("p (t c) -> p t c", c=P), AX_X, ALU.add))
                dve.tensor_scalar(g_st[:, 0, :], g_st[:, 0, :], 1.0 / P, EPS, ALU.mult, ALU.add).then_inc(G["ms"], 1)
                flatG = g_G[:].rearrange("p t c -> p (t c)")
                od.then(dve.tensor_tensor(g_D[:], g_D[:], flatG, ALU.mult))
                dve.wait_ge(G["rs"], h + 1)
                oh = g_D[:].rearrange("p (t c) -> p t c", c=P)
                od.then(dve.tensor_tensor(oh, oh, g_st[:, 1, :].unsqueeze(2).broadcast_to([P, NT, P]), ALU.mult))
                dve.tensor_tensor(X[:, :, bass.ds(h * P + SBW, P)], oh,
                                  g_gain[:, bass.ds(h * P, P)].unsqueeze(1).broadcast_to([P, NT, P]),
                                  ALU.mult).then_inc(G["x"], 1)
                dve.wait_ge(G["x"], h + 1)
                dve.wait_ge(G["st"], h * 32 + 32)
            od.leave(HG_HEADS)

        def hg_pool(pool):
            with pool.Fori(0, HG_HEADS) as h:
                pool.wait_ge(G["ms"], h + 1)
                pool.tensor_tensor(g_st[:, 1, :], g_st[:, 0, :], half[:], ALU.pow)\
                    .then_inc(G["rs"], 1)

        def add_out(tag):
            return sem(f"{tag}_y"), sem(f"{tag}_add")

        def out_pe(pe, sems, round0, op_hi, op_lo, nkb, per_half, banks=(0, 1)):
            y, add = sems
            n = 0
            for half_ in range(2):
                units = [(round0 + (half_ * per_half + j) // SLOTS, (half_ * per_half + j) % SLOTS)
                         for j in range(per_half)]
                for c, s in units:
                    wait_unit(pe, unit(c, s), s)
                for t in range(NT):
                    if n >= 2:
                        pe.wait_ge(add, n - 1)
                    out = PS[:, banks[n % 2], :]
                    tok = slice(t * P, (t + 1) * P)
                    for kb in range(nkb):
                        s = units[kb // 2][1]
                        cols = slice((kb % 2) * 512, (kb % 2 + 1) * 512)
                        pe.matmul(out, op_hi[:, kb, tok], w_hi[s][:, cols], start=kb == 0, stop=False)
                        pe.matmul(out, op_lo[:, kb, tok], w_hi[s][:, cols], start=False, stop=False)
                        last = pe.matmul(out, op_hi[:, kb, tok], w_lo[s][:, cols], start=False, stop=kb == nkb - 1)
                        if t == NT - 1 and kb % 2:
                            last.then_inc(slot_free[s], 1)
                    if t < NT - 1:
                        last.then_inc(y, 1)
                    n += 1

        def out_dve(dve, sems, round0, per_half, banks=(0, 1), between=None):
            y, add = sems
            n = 0
            for half_ in range(2):
                for t in range(NT):
                    if t < NT - 1:
                        dve.wait_ge(y, half_ * (NT - 1) + t + 1)
                    else:
                        end = half_ * per_half + per_half - 1
                        projected(dve, unit(round0 + end // SLOTS, end % SLOTS), end % SLOTS)
                    x = X[:, t, half_ * 512:(half_ + 1) * 512]
                    dve.tensor_tensor(x, PS[:, banks[n % 2], :], x, ALU.add).then_inc(add, 1)
                    n += 1
                if between:
                    between(half_)

        m_ev, m_tr, m_tev, m_st = (sem("m_" + x) for x in ("ev", "tr", "tev", "st"))
        mt_ = c_KT[:].rearrange("p s k -> p (s k)")

        def mem_pe(pe):
            for j in range(8):
                c, s = R_MEM + j // 4, j % 4
                wait_unit(pe, unit(c, s), s)
                if j >= 2:
                    pe.wait_ge(m_ev, j - 1)
                project(pe, s, j % 2, NMEM, NMEM)
            for j in range(8):
                pe.wait_ge(m_ev, j + 1)
                if j >= 2:
                    pe.wait_ge(m_tev, j - 1)
                src = c_kT[:, j, :] if j < 4 else mt_[:, (j - 4) * NMEM:(j - 3) * NMEM]
                for t in range(2):
                    last = pe.transpose(PS[:, 2 + j % 2, t * P:(t + 1) * P], src[:, t * P:(t + 1) * P], ident)
                last.then_inc(m_tr, 1)

        def mem_act(act):
            for j in range(8):
                projected(act, unit(R_MEM + j // 4, j % 4), j % 4)
                dst = c_kT[:, j, :] if j < 4 else mt_[:, (j - 4) * NMEM:(j - 3) * NMEM]
                act.activation(dst, PS[:, j % 2, 0:NMEM], ACT.Copy).then_inc(m_ev, 1)
                if j < 4:
                    cut_hi_unit(act, unit(R_MEM + 1, j), j)
                else:
                    cut_hi_unit(act, unit(R_MQ, j - 4), j - 4)

        def mem_dve(dve):
            for j in range(8):
                if j < 4:
                    cut_lo_unit(dve, unit(R_MEM + 1, j), j)
                else:
                    cut_lo_unit(dve, unit(R_MQ, j - 4), j - 4)
            for j in range(8):
                dve.wait_ge(m_tr, j + 1)
                dst = xn[:, 0, :].rearrange("p (t c) -> p t c", t=2) if j < 4 else c_v[:]
                dve.tensor_copy(dst[:, :, (j % 4) * P:(j % 4 + 1) * P],
                                PS[:, 2 + j % 2, 0:NMEM].rearrange("p (t c) -> p t c", t=2)).then_inc(m_tev, 1)

        c_ev = sem("c_ev")
        CN = {n: sem("c_" + n) for n in
              "z max nb ex rc p tr te av hi lo kt ke prep ko QB dv ldK ldV vfree".split()}
        units_c = [(hd, t) for hd in range(MEM_HEADS) for t in range(NT)]
        NU = len(units_c)

        def mq_pe(pe):
            for j in range(4):
                wait_unit(pe, unit(R_MQ, j), j)
                if j >= 2:
                    pe.wait_ge(c_ev, j - 1)
                project(pe, j, 3 * (j % 2))

        def mq_act(act):
            for j in range(4):
                projected(act, unit(R_MQ, j), j)
                act.activation(as3(c_q[:, j, :]), bank3(3 * (j % 2)), ACT.Copy).then_inc(c_ev, 1)
                cut_hi_unit(act, unit(R_MO, j), j)

        def mq_dve(dve):
            for j in range(4):
                cut_lo_unit(dve, unit(R_MO, j), j)

        ogroups = [(hd, t0, min(4, NT - t0)) for hd in range(MEM_HEADS) for t0 in (0, 4, 8)]

        def cross_pe(pe):
            pe.wait_ge(c_ev, 4)

            def z(n):
                hd, t = units_c[n]
                if n >= 2:
                    pe.wait_ge(CN["ex"], n - 1)
                if t < SMP:
                    pe.matmul(PS[:, n % 2, 0:NMEM], c_q[:, hd, t * P:(t + 1) * P], c_kT[:, hd, :],
                              start=True, stop=True).then_inc(CN["z"], 1)
                    return
                for g in range(2):
                    pe.wait_ge(CN["ldK"], 16 * (2 * hd + g) + 16)
                    for b in range(2):
                        kc = (2 * hd + g) * 2 + b
                        if kc >= 2:
                            pe.wait_ge(CN["ke"], kc - 1)
                        for j in range(4):
                            last = pe.transpose(PS[:, 6 + b, j * P:(j + 1) * P],
                                                xn[:, 0, :].rearrange("p (b c) -> p b c", c=P)[:, 4 * b + j, :], ident)
                        last.then_inc(CN["kt"], 1)
                    pe.wait_ge(CN["ke"], (2 * hd + g) * 2 + 2)
                    if g == 0:
                        pe.wait_ge(CN["QB"], hd + 1)
                    for s in range(4):
                        last = pe.matmul(PS[:, n % 2, 0:NMEM], c_QB[:, (4 * g + s) * P:(4 * g + s + 1) * P],
                                         c_KT[:, s, :], start=g == 0 and s == 0, stop=g == 1 and s == 3)
                    if g == 0:
                        last.then_inc(CN["ko"], 1)
                last.then_inc(CN["z"], 1)

            def transposes(n):
                pe.wait_ge(CN["p"], n + 1)
                if n >= 2:
                    pe.wait_ge(CN["te"], n - 1)
                for j in range(2):
                    last = pe.transpose(PS[:, 2 + n % 2, j * P:(j + 1) * P], c_P[:, n % 2, j * P:(j + 1) * P], ident)
                last.then_inc(CN["tr"], 1)

            def av(n):
                hd, t = units_c[n]
                grp = hd * 3 + t // 4
                if t % 4 == 0 and grp >= 2:
                    pe.wait_ge(CN["lo"], grp - 1)
                out = PS[:, 4 + grp % 2, (t % 4) * P:(t % 4 + 1) * P]
                pe.wait_ge(CN["te"], n + 1)
                if t < SMP:
                    for kt in range(2):
                        last = pe.matmul(out, c_v[:, kt, hd * P:(hd + 1) * P], c_PT[:, n % 2, kt * P:(kt + 1) * P],
                                         start=kt == 0, stop=kt == 1)
                else:
                    for g in range(2):
                        pe.wait_ge(CN["ldV"], 16 * (2 * hd + g) + 16)
                        V = xn[:, 1, :].rearrange("p (b c) -> p b c", c=P) if g == 0 else c_V1[:]
                        for s in range(4):
                            sc = slice((4 * g + s) * NQ, (4 * g + s + 1) * NQ)
                            for kt in range(2):
                                last = pe.matmul(out[:, sc], V[:, 2 * s + kt, :],
                                                 c_PT[:, n % 2, kt * P:(kt + 1) * P][:, sc],
                                                 start=kt == 0, stop=kt == 1)
                last.then_inc(CN["av"], 1)

            z(0)
            for n in range(NU):
                if n + 1 < NU:
                    z(n + 1)
                transposes(n)
                av(n)

        def cross_act(act):
            def ex(n):
                act.wait_ge(CN["nb"], n + 1)
                if n >= 2:
                    act.wait_ge(CN["tr"], n - 1)
                act.activation(c_P[:, n % 2, :], PS[:, n % 2, 0:NMEM], ACT.Exp, bias=c_st[:, 1, n:n + 1],
                               scale=P ** -0.5, accum_out=c_st[:, 2, n:n + 1]).then_inc(CN["ex"], 1)

            def keys(n):
                hd = units_c[n][0]
                for kc in range(4):
                    k = hd * 4 + kc
                    act.wait_ge(CN["kt"], k + 1)
                    if kc == 0 and hd > 0:
                        act.wait_ge(CN["z"], n - NT + 1)
                    if kc == 2:
                        act.wait_ge(CN["ko"], hd + 1)
                    act.activation(c_KT[:, 2 * (kc % 2):2 * (kc % 2) + 2, :],
                                   PS[:, 6 + kc % 2, :].rearrange("p (s k) -> p s k", s=2), ACT.Copy)\
                       .then_inc(CN["ke"], 1)

            ex(0)
            for n in range(NU):
                if n + 1 < NU:
                    if units_c[n + 1][1] == SMP:
                        keys(n + 1)
                    ex(n + 1)
                act.wait_ge(CN["tr"], n + 1)
                if n >= 2:
                    act.wait_ge(CN["av"], n - 1)
                act.activation(c_PT[:, n % 2, :], PS[:, 2 + n % 2, 0:NMEM], ACT.Copy).then_inc(CN["te"], 1)
                hd, t = units_c[n]
                if t in (3, 7, 8):
                    _, t0, nt = ogroups[hd * 3 + t // 4]
                    act.wait_ge(CN["av"], n + 1)
                    act.activation(h_hi[:, hd, t0 * P:(t0 + nt) * P], PS[:, 4 + (hd * 3 + t // 4) % 2, 0:nt * P],
                                   ACT.Copy).then_inc(CN["hi"], 1)

        def cross_dve(dve):
            dve.wait_ge(c_ev, 4)
            od = Order(dve, CN["dv"])
            od.then(dve.memset(c_QB[:], 0.0))

            def bias(n):
                hd, t = units_c[n]
                if t == SMP:
                    if hd > 0:
                        dve.wait_ge(CN["z"], n - NT + 1)
                    dve.tensor_copy(c_QB[:].rearrange("p (s c) -> p s c", c=P + NQ)[:, :, 0:NQ],
                                    c_q[:, hd, SEQ:T].rearrange("p (s c) -> p s c", c=NQ)).then_inc(CN["QB"], 1)
                dve.wait_ge(CN["z"], n + 1)
                dve.reduce_max(c_st[:, 0, n:n + 1], PS[:, n % 2, 0:NMEM], AX_X).then_inc(CN["max"], 1)
                dve.wait_ge(CN["max"], n + 1)
                dve.tensor_scalar(c_st[:, 1, n:n + 1], c_st[:, 0, n:n + 1], -(P ** -0.5), None, ALU.mult)\
                   .then_inc(CN["nb"], 1)

            bias(0)
            for n in range(NU):
                if n + 1 < NU:
                    bias(n + 1)
                dve.wait_ge(CN["ex"], n + 1)
                dve.reciprocal(c_st[:, 3, n:n + 1], c_st[:, 2, n:n + 1]).then_inc(CN["rc"], 1)
                dve.wait_ge(CN["rc"], n + 1)
                dve.tensor_scalar(c_P[:, n % 2, :], c_P[:, n % 2, :], c_st[:, 3, n:n + 1], None, ALU.mult)\
                   .then_inc(CN["p"], 1)
                if n >= 2:
                    m = n - 2
                    if units_c[m][1] in (3, 7, 8):
                        low(m)
            for m in (NU - 2, NU - 1):
                if units_c[m][1] in (3, 7, 8):
                    low_(dve, m)

        def low_(dve, n):
            hd, t = units_c[n]
            grp = hd * 3 + t // 4
            _, t0, nt = ogroups[grp]
            dve.wait_ge(CN["hi"], grp + 1)
            dve.tensor_tensor(h_lo[:, hd, t0 * P:(t0 + nt) * P], PS[:, 4 + grp % 2, 0:nt * P],
                              h_hi[:, hd, t0 * P:(t0 + nt) * P].bitcast(F32), ALU.subtract).then_inc(CN["lo"], 1)

        def low(n):
            low_(nc.vector, n)

        f_rl, f_hi, f_sq, f_lo, f_y, f_add = (sem("f_" + x) for x in ("rl", "hi", "sq", "lo", "y", "add"))

        def ff_round(g, second):
            return R_FF + g * 2 + second

        def ff_loop(eng, body):
            with eng.Fori(0, FG - 1) as g:
                body(g, False)
            body(FG - 1, True)

        def ff_pe(pe):
            def body(g, last_turn):
                for b in range(FB):
                    wait_unit(pe, unit(ff_round(g, 0), b), b)
                    if b >= 2:
                        pe.wait_ge(f_rl, g * FB + b - 1)
                    project(pe, b, 3 * (b % 2))
                for half_ in range(2):
                    for s in (2 * half_, 2 * half_ + 1):
                        wait_unit(pe, unit(ff_round(g, 1), s), s)
                    for t in range(NT):
                        n = half_ * NT + t
                        if n >= 2:
                            pe.wait_ge(f_add, g * 2 * NT + n - 1)
                        for b in range(FB):
                            if n == 0:
                                pe.wait_ge(f_lo, g * FB + b + 1)
                            s = 2 * half_ + b // 2
                            cols = slice((b % 2) * 512, (b % 2 + 1) * 512)
                            tok = slice(t * P, (t + 1) * P)
                            out = PS[:, 6 + n % 2, :]
                            pe.matmul(out, u_hi[:, b, tok], w_hi[s][:, cols], start=b == 0, stop=False)
                            pe.matmul(out, u_lo[:, b, tok], w_hi[s][:, cols], start=False, stop=False)
                            last = pe.matmul(out, u_hi[:, b, tok], w_lo[s][:, cols], start=False, stop=b == FB - 1)
                            if t == NT - 1 and b % 2:
                                last.then_inc(slot_free[s], 1)
                        if t < NT - 1:
                            last.then_inc(f_y, 1)
                pe.wait_ge(f_add, g * 2 * NT + 2 * NT)

            ff_loop(pe, body)

        def ff_act(act):
            def body(g, last_turn):
                for b in range(FB):
                    projected(act, unit(ff_round(g, 0), b), b)
                    if b:
                        act.wait_ge(f_sq, g * FB + b)
                        act.wait_ge(f_hi, g * FB + b)
                    act.activation(as3(f_r[:]), bank3(3 * (b % 2)), ACT.Relu).then_inc(f_rl, 1)
                    act.wait_ge(f_rl, g * FB + b + 1)
                    act.activation(u_hi[:, b, :], f_r[:], ACT.Square).then_inc(f_hi, 1)
                    cut_hi_unit(act, unit(ff_round(g, 1), b), b)
                act.wait_ge(f_sq, g * FB + FB)
                if not last_turn:
                    for b in range(FB):
                        cut_hi_unit(act, unit(ff_round(g, 2), b), b)

            ff_loop(act, body)

        def ff_dve(dve):
            def body(g, last_turn):
                for b in range(FB):
                    dve.wait_ge(f_rl, g * FB + b + 1)
                    if b:
                        dve.wait_ge(f_lo, g * FB + b)
                    dve.tensor_tensor(f_s, f_r[:], f_r[:], ALU.mult).then_inc(f_sq, 1)
                    dve.wait_ge(f_sq, g * FB + b + 1)
                    dve.wait_ge(f_hi, g * FB + b + 1)
                    dve.tensor_tensor(u_lo[:, b, :], f_s, u_hi[:, b, :].bitcast(F32), ALU.subtract)\
                       .then_inc(f_lo, 1)
                    cut_lo_unit(dve, unit(ff_round(g, 1), b), b)
                dve.wait_ge(f_lo, g * FB + FB)
                for half_ in range(2):
                    for t in range(NT):
                        n = half_ * NT + t
                        if t < NT - 1:
                            dve.wait_ge(f_y, g * 2 * (NT - 1) + half_ * (NT - 1) + t + 1)
                        else:
                            projected(dve, unit(ff_round(g, 1), 2 * half_ + 1), 2 * half_ + 1)
                        x = X[:, t, half_ * 512:(half_ + 1) * 512]
                        dve.tensor_tensor(x, PS[:, 6 + n % 2, :], x, ALU.add).then_inc(f_add, 1)
                    if not last_turn:
                        for s in (2 * half_, 2 * half_ + 1):
                            cut_lo_unit(dve, unit(ff_round(g, 2), s), s)
                dve.wait_ge(f_add, g * 2 * NT + 2 * NT)

            ff_loop(dve, body)

        xl = [sem(f"x_in{t}") for t in range(NT)]
        ml = [sem(f"mem_in{t}") for t in range(2)]
        wo_s, mo_s = add_out("wo"), add_out("mo")
        xrow = lambda t: X[:, t, :]
        mrow = lambda t: c_q[:, t, 0:D]
        n_mix = Norm("mix", NT, D, xrow, loads=xl)
        n_sb = Norm("sb", NT, SBW, xrow)
        n_mem = Norm("mem", 2, D, mrow, loads=ml)
        n_mq = Norm("mq", NT, D, xrow)
        n_ff = Norm("ff", NT, D, xrow)
        n_fin = Norm("fin", NT, D, xrow, final=True)
        for g_at, n in enumerate((n_mix, n_sb, n_mem, n_mq, n_ff, n_fin)):
            n.gain_at = g_at + 1
        B_MIX, B_SB, B_HG, B_MN, B_WO, B_MEM, B_MQN, B_CR, B_MO, B_FN, B_FF, B_FIN = range(1, 13)
        xrl = sem("x_again")

        def cache_load_to(sp, dst, src, g, col, s_):
            x = src.rearrange("s (t q) c -> q (s t) c", q=P)[:, 8 * g:8 * g + 8, col:col + P]
            sp.dma_start(dst, x).then_inc(s_, 16)

        def row_unit(sp, s, n, w, row, half_):
            settle(sp)
            sp.wait_ge(cut_lo[s % 2], n)
            sp.dma_start(raw[s % 2][:].rearrange("p (k c) -> p k c", k=2),
                         w[bass.ds(row, 2 * P), half_ * 512:(half_ + 1) * 512]
                         .rearrange("(k p) c -> p k c", p=P)).then_inc(landed[s % 2], 16)

        block = ctx.enter_context(nc.Block())

        @block.sync
        def _(sp):
            def load_gain(src, n):
                sp.dma_start(gain[:, 0:n], src.rearrange("(a n) -> a n", a=1).broadcast_to([P, n]))\
                  .then_inc(ld("gain"), 16)

            def feature_unit(s, n, w, col):
                if not isinstance(n, int) or n > 0:
                    settle(sp)
                    sp.wait_ge(cut_lo[s % 2], n)
                sp.dma_start(raw[s % 2][:].rearrange("p (k c) -> p k c", k=KB),
                             w.rearrange("(k p) c -> p k c", p=P)[:, :, bass.ds(col, P)]).then_inc(landed[s % 2], 16)

            def column_unit(s, n, w, kb, half_):
                sp.wait_ge(cut_lo[s % 2], n)
                sp.dma_start(raw[s % 2][:].rearrange("p (k c) -> p k c", k=2),
                             w[bass.ds(kb * P, 2 * P), half_ * 512:(half_ + 1) * 512]
                             .rearrange("(k p) c -> p k c", p=P)).then_inc(landed[s % 2], 16)

            sp.dma_start(cst[:], a["cst"]).then_inc(ld("cst"), 16)
            sp.dma_start(c_q[:, 0, 0:(len(LEVELS) + 1) * P], a["lvl"].rearrange("p n c -> p (n c)")).then_inc(ld("cst"), 16)
            for t in range(NT):
                src = a["x_prompt"][t * P:(t + 1) * P, :] if t < SMP else a["x_sample"]
                sp.dma_start(X[:, t, :], src).then_inc(xl[t], 16)
                if t == 0:
                    load_gain(a["norm_mix"], D)
            for s in range(3):
                feature_unit(s, unit_sb(0, s)[1], a["w_in"], s * SBW)

            def pair_io(p):
                col = sp.snap(p * P) if not isinstance(p, int) else p * P
                for g in range(2):
                    settle(sp)
                    if g == 0:
                        sp.wait_ge(sb_kT, p + 1)
                    else:
                        sp.wait_ge(sb_tc, p * NC + of_K[0][-1] + 1)
                    cache_load(s_cK, a["cache_sb_k"], g, col, sb_cK)
                    if g == 1:
                        settle(sp)
                        sp.wait_ge(sb_av, p * NAV + 25)
                    cache_load(s_cV, a["cache_sb_v"], g, col, sb_cV)
                    if g == 0:
                        for buf, done, dp, ds_ in ((s_k, sb_k, o["kp"], o["ks"]), (s_v, sb_v, o["vp"], o["vs"])):
                            settle(sp)
                            sp.wait_ge(done, p * 3 + 3)
                            sp.dma_start(dp.rearrange("(t p) c -> p t c", p=P)[:, :, bass.ds(col, P)],
                                         buf[:, 0:SMP, :]).then_inc(sb_st, 16)
                            sp.dma_start(ds_[:, bass.ds(col, P)], buf[:, SMP, :]).then_inc(sb_st, 16)

            def cache_load(buf, src, g, col, s_):
                x = src.rearrange("s (t q) c -> q (s t) c", q=P)[:, 8 * g:8 * g + 8, :]
                sp.dma_start(buf[:], x[:, :, bass.ds(col, P)]).then_inc(s_, 16)

            sp.wait_ge(bar, ENGINES * B_MIX)
            with sp.Fori(0, PAIRS - 1) as p:
                cols = [sp.snap(p * P + P + s * SBW) for s in range(3)]
                for s in range(3):
                    feature_unit(s, unit_sb(p + 1, s)[1], a["w_in"], cols[s])
                pair_io(p)
            for s in range(3):
                feature_unit(s, unit(0, s)[1], a["w_in"], 3 * SBW + s * HGW)
            pair_io(PAIRS - 1)
            feature_unit(3, unit(0, 3)[1], a["w_in"], 3 * SBW + 3 * HGW)
            sp.wait_ge(bar, ENGINES * B_SB)
            sp.dma_start(g_keep[:], a["keep"]).then_inc(ld("keep"), 16)
            sp.dma_start(g_gain[:], a["hg_gain"].rearrange("(a n) -> a n", a=1).broadcast_to([P, HGW]))\
              .then_inc(ld("keep"), 16)

            def head_io(h):
                settle(sp)
                sp.wait_ge(G["q"], h + 1)
                sp.dma_start(g_S0[:], a["state"][:, bass.ds(h, 1), :, :].rearrange("s a k v -> k (s a) v"))\
                  .then_inc(G["s0"], 16)

            def head_out(h):
                settle(sp)
                sp.wait_ge(G["s"], h * SMP + SMP)
                sp.dma_start(o["sp"][bass.ds(h, 1)].rearrange("a k v -> k (a v)"), g_S[:, SMP - 1, :])\
                  .then_inc(G["st"], 16)
                settle(sp)
                sp.wait_ge(G["sout"], h + 1)
                sp.dma_start(o["ss"][:, bass.ds(h, 1), :, :].rearrange("s a k v -> k (s a) v"), g_S0[:])\
                  .then_inc(G["st"], 16)

            with sp.Fori(0, HG_HEADS - 1) as h:
                cols = [sp.snap(h * P + P + 3 * SBW + s * HGW) for s in range(4)]
                hh = sp.snap(h + 0)
                head_io(h)
                for s in range(4):
                    feature_unit(s, unit(h + 1, s)[1], a["w_in"], cols[s])
                head_out(h)
            head_io(HG_HEADS - 1)
            for s in range(4):
                column_unit(s, unit(R_OUT, s)[1], a["w_out"], 2 * s, 0)
            head_out(HG_HEADS - 1)
            sp.wait_ge(bar, ENGINES * B_HG)
            load_gain(a["sb_gain"], SBW)
            sp.wait_ge(bar, ENGINES * B_MN)
            for t in range(NT):
                src = a["x_prompt"][t * P:(t + 1) * P, :] if t < SMP else a["x_sample"]
                sp.dma_start(X[:, t, :], src).then_inc(xrl, 16)
            load_gain(a["norm_mem_kv"], D)
            for t in range(2):
                sp.dma_start(c_q[:, t, 0:D], a["mem"][t * P:(t + 1) * P, :]).then_inc(ml[t], 16)
            for s in range(4):
                column_unit(s, unit(R_OUT + 1, s)[1], a["w_out"], 2 * s, 1)
            for s in range(4):
                feature_unit(s, unit(R_MEM, s)[1], a["w_mk"], s * P)
            for s in range(4):
                feature_unit(s, unit(R_MEM + 1, s)[1], a["w_mv"], s * P)
            for s in range(4):
                feature_unit(s, unit(R_MQ, s)[1], a["w_mq"], s * P)
            sp.wait_ge(m_tev, 4)
            sp.dma_start(o["mk"].rearrange("(t p) c -> p t c", p=P), xn[:, 0, :].rearrange("p (t c) -> p t c", t=2))\
              .then_inc(m_st, 16)
            sp.wait_ge(m_tev, 8)
            sp.dma_start(o["mv"].rearrange("(t p) c -> p t c", p=P), c_v[:]).then_inc(m_st, 16)
            sp.wait_ge(m_st, 32)
            sp.wait_ge(bar, ENGINES * B_MEM)
            load_gain(a["norm_mem_q"], D)
            for s in range(4):
                column_unit(s, unit(R_MO, s)[1], a["w_mo"], 2 * (s % 2), s // 2)
            sp.wait_ge(bar, ENGINES * B_MQN)
            for hd in range(MEM_HEADS):
                for g in range(2):
                    n = 2 * hd + g
                    if n:
                        sp.wait_ge(CN["kt"], 2 * n)
                    cache_load_to(sp, xn[:, 0, :].rearrange("p (b c) -> p b c", c=P), a["cache_mem_k"], g, hd * P,
                                  CN["ldK"])
                    if hd:
                        sp.wait_ge(CN["av"], hd * NT)
                    dst = xn[:, 1, :].rearrange("p (b c) -> p b c", c=P) if g == 0 else c_V1[:]
                    cache_load_to(sp, dst, a["cache_mem_v"], g, hd * P, CN["ldV"])
            for s in range(4):
                feature_unit(s, unit(ff_round(0, 0), s)[1], a["w_ffn1"], s * P)
            sp.wait_ge(bar, ENGINES * B_MO)
            load_gain(a["norm_ffn"], D)
            with sp.Fori(0, FG - 1) as g:
                cols = [sp.snap(g * (FB * P) + FB * P + s * P) for s in range(4)]
                kbs = [sp.snap(g * (FB * P) + (s % 2) * 2 * P) for s in range(4)]
                for s in range(4):
                    row_unit(sp, s, unit(ff_round(g, 1), s)[1], a["w_ffn2"], kbs[s], s // 2)
                for s in range(4):
                    feature_unit(s, unit(ff_round(g, 2), s)[1], a["w_ffn1"], cols[s])
            for s in range(4):
                row_unit(sp, s, unit(ff_round(FG - 1, 1), s)[1], a["w_ffn2"],
                         (FG - 1) * FB * P + (s % 2) * 2 * P, s // 2)
            sp.wait_ge(bar, ENGINES * B_FF)
            load_gain(a["norm_final"], D)
            for t in range(NT):
                sp.wait_ge(N["xn"], n_fin.base + t + 1)
                dst = o["yp"][t * P:(t + 1) * P, :] if t < SMP else o["ys"]
                sp.dma_start(dst, xn[:, t % 2, :]).then_inc(N["out"], 16)
                sp.wait_ge(N["out"], 16 * (t + 1))

        @block.gpsimd
        def _(pool):
            pool.memset(half[:], -0.5).then_inc(ld("half"), 1)
            pool.wait_ge(ld("half"), 1)
            norm_pool(pool, n_mix)
            barrier(pool, B_MIX)
            barrier(pool, B_SB)
            hg_pool(pool)
            barrier(pool, B_HG)
            norm_pool(pool, n_sb)
            barrier(pool, B_MN)
            barrier(pool, B_WO)
            norm_pool(pool, n_mem)
            barrier(pool, B_MEM)
            norm_pool(pool, n_mq)
            barrier(pool, B_MQN)
            barrier(pool, B_CR)
            barrier(pool, B_MO)
            norm_pool(pool, n_ff)
            barrier(pool, B_FN)
            barrier(pool, B_FF)
            norm_pool(pool, n_fin)

        @block.tensor
        def _(pe):
            for s in range(SLOTS):
                pe.sem_inc(slot_free[s], 1)
            pe.wait_ge(ld("cst"), 32)
            norm_pe(pe, n_mix)
            barrier(pe, B_MIX)
            sb_pe(pe)
            barrier(pe, B_SB)
            hg_pe(pe)
            barrier(pe, B_HG)
            norm_pe(pe, n_sb)
            barrier(pe, B_MN)
            out_pe(pe, wo_s, R_OUT, h_hi, h_lo, KB, 4)
            barrier(pe, B_WO)
            norm_pe(pe, n_mem)
            pe.wait_ge(N["lo"], 2 * (n_mem.base + 2))
            mem_pe(pe)
            barrier(pe, B_MEM)
            norm_pe(pe, n_mq)
            barrier(pe, B_MQN)
            mq_pe(pe)
            cross_pe(pe)
            barrier(pe, B_CR)
            out_pe(pe, mo_s, R_MO, h_hi, h_lo, 4, 2)
            barrier(pe, B_MO)
            norm_pe(pe, n_ff)
            barrier(pe, B_FN)
            ff_pe(pe)
            barrier(pe, B_FF)

        @block.scalar
        def _(act):
            act.preload_act_table_set("natural_log_exp_and_others")
            norm_act(act, n_mix)
            for s in range(3):
                cut_hi_unit(act, unit_sb(0, s), s)
            barrier(act, B_MIX)
            sb_act(act)
            cut_hi_unit(act, unit(0, 3), 3)
            barrier(act, B_SB)
            hg_act(act)
            barrier(act, B_HG)
            norm_act(act, n_sb)
            barrier(act, B_MN)
            for s in range(4):
                cut_hi_unit(act, unit(R_OUT + 1, s), s)
            for s in range(4):
                cut_hi_unit(act, unit(R_MEM, s), s)
            barrier(act, B_WO)
            norm_act(act, n_mem)
            mem_act(act)
            barrier(act, B_MEM)
            act.wait_ge(m_st, 32)
            norm_act(act, n_mq)
            barrier(act, B_MQN)
            mq_act(act)
            cross_act(act)
            barrier(act, B_CR)
            for s in range(4):
                cut_hi_unit(act, unit(ff_round(0, 0), s), s)
            barrier(act, B_MO)
            norm_act(act, n_ff)
            barrier(act, B_FN)
            ff_act(act)
            barrier(act, B_FF)
            norm_act(act, n_fin)

        @block.vector
        def _(dve):
            dve.wait_ge(ld("cst"), 32)
            dve.tensor_copy(lvl[:].rearrange("p n c -> p (n c)"), c_q[:, 0, 0:(len(LEVELS) + 1) * P])
            norm_dve(dve, n_mix)
            for s in range(3):
                cut_lo_unit(dve, unit_sb(0, s), s)
            dve.wait_ge(ld("cst"), 32)
            barrier(dve, B_MIX)
            sb_dve(dve)
            cut_lo_unit(dve, unit(0, 3), 3)
            barrier(dve, B_SB)
            dve.wait_ge(ld("keep"), 32)
            hg_dve(dve)
            barrier(dve, B_HG)
            norm_dve(dve, n_sb)
            barrier(dve, B_MN)
            dve.wait_ge(xrl, 16 * NT)

            def between(half_):
                for s in range(4):
                    cut_lo_unit(dve, unit(R_OUT + 1 + half_, s), s)

            out_dve(dve, wo_s, R_OUT, 4, between=between)
            barrier(dve, B_WO)
            norm_dve(dve, n_mem)
            mem_dve(dve)
            barrier(dve, B_MEM)
            norm_dve(dve, n_mq)
            barrier(dve, B_MQN)
            mq_dve(dve)
            cross_dve(dve)
            barrier(dve, B_CR)

            def between_mo(half_):
                for s in (2 * half_, 2 * half_ + 1):
                    cut_lo_unit(dve, unit(ff_round(0, 0), s), s)

            out_dve(dve, mo_s, R_MO, 2, between=between_mo)
            barrier(dve, B_MO)
            norm_dve(dve, n_ff)
            barrier(dve, B_FN)
            ff_dve(dve)
            barrier(dve, B_FF)
            norm_dve(dve, n_fin)


_INS = {
    "x_prompt": (SEQ, D), "x_sample": (NS * NQ, D), "mem": (NMEM, D),
    "cache_sb_k": (NS, PAST, SBW), "cache_sb_v": (NS, PAST, SBW), "state": (NS, HG_HEADS, P, P),
    "cache_mem_k": (NS, NMEM, MEMW), "cache_mem_v": (NS, NMEM, MEMW),
    "norm_mix": (D,), "w_in": (D, 3 * SBW + 4 * HGW), "sb_gain": (SBW,), "hg_gain": (HGW,),
    "w_out": (SBW + HGW, D), "norm_mem_q": (D,), "norm_mem_kv": (D,), "w_mq": (D, MEMW), "w_mk": (D, MEMW),
    "w_mv": (D, MEMW), "w_mo": (MEMW, D), "norm_ffn": (D,), "w_ffn1": (D, DFF), "w_ffn2": (DFF, D),
    "norm_final": (D,),
}
_FROM = {"mem": "mem_prompt", "state": "state_hgrn"}
_OUTS = [
    ("yp", (SEQ, D), (1, SEQ, D)), ("ys", (NS * NQ, D), (NS, NQ, D)),
    ("kp", (SEQ, SBW), (1, 1, SEQ, 8, HD)), ("vp", (SEQ, SBW), (1, 1, SEQ, 8, HD)),
    ("sp", (HG_HEADS, P, P), (1, 1, HG_HEADS, P, P)),
    ("mk", (NMEM, MEMW), (1, 1, NMEM, MEM_HEADS, P)), ("mv", (NMEM, MEMW), (1, 1, NMEM, MEM_HEADS, P)),
    ("ks", (NS * NQ, SBW), (1, NS, NQ, 8, HD)), ("vs", (NS * NQ, SBW), (1, NS, NQ, 8, HD)),
    ("ss", (NS, HG_HEADS, P, P), (1, NS, HG_HEADS, P, P)),
]


def kernel(**inputs):
    import numpy as np
    import concourse.bacc as bacc
    from concourse.bass_utils import run_bass_kernel_spmd

    nc = bacc.Bacc("TRN2", target_bir_lowering=False, num_devices=1)
    cst, lvl, keep = shape_constants()
    arrays = {"cst": cst, "lvl": lvl, "keep": keep}
    for name, shape in _INS.items():
        arrays[name] = np.ascontiguousarray(inputs[_FROM.get(name, name)]).reshape(shape)
    a = {name: nc.dram_tensor(name, x.shape, mybir.dt.from_np(x.dtype), kind="ExternalInput").ap()
         for name, x in arrays.items()}
    o = {name: nc.dram_tensor("out_" + name, shape, F32, kind="ExternalOutput").ap() for name, shape, _ in _OUTS}
    build(nc, a, o)
    r = run_bass_kernel_spmd(nc, [arrays], core_ids=[0])
    return tuple(r.results[0]["out_" + name].reshape(shape) for name, _, shape in _OUTS)
```

```python
from contextlib import ExitStack

import concourse.bass as bass
from concourse import mybir

F32 = mybir.dt.float32
F32R = mybir.dt.float32r
U8 = mybir.dt.uint8
ALU = mybir.AluOpType
ACT = mybir.ActivationFunctionType
AX_X = mybir.AxisListType.X

P = 128
D = 1024
KB = D // P
SEQ = 1024
NS, NQ = 8, 16
PAST = 256
NT = SEQ // P + 1
SMP = NT - 1
T = NT * P
TG = T // 3
SBW, HGW, MEMW = 512, 512, 512
HD = 64
PAIRS = SBW // P
HG_HEADS = HGW // P
NMEM = 256
MEM_HEADS = MEMW // P
DFF = 4 * D
FB = 4
FG = DFF // P // FB
EPS = 1e-6
CAP = 40.0
LEVELS = [1, 2, 4, 8, 16, 32, 64]
SLOTS = 4
RAWS = 2

C_ID, C_TRI, C_NEG, C_TRI16, C_NEG16, C_BLK, C_STR, C_ONE = 0, 128, 256, 384, 400, 416, 672, 680
C_END = 681


def shape_constants():
    import numpy as np

    p = np.arange(P)[:, None]
    f = np.arange(P)[None, :]
    j = np.arange(NQ)[None, :]
    cst = np.zeros((P, C_END), np.float32)
    cst[:, C_ID:C_ID + P] = p == f
    cst[:, C_TRI:C_TRI + P] = f < p
    cst[:, C_NEG:C_NEG + P] = np.where(f < p, 0.0, -1e30)
    cst[:, C_TRI16:C_TRI16 + NQ] = j < p % NQ
    cst[:, C_NEG16:C_NEG16 + NQ] = np.where(j < p % NQ, 0.0, -1e30)
    for g in range(2):
        own = np.arange(NS)[None, :] == g * 4 + p // 32
        cst[:, C_BLK + g * P:C_BLK + (g + 1) * P] = np.repeat(own, NQ, 1)
    cst[:, C_STR:C_STR + NS] = np.arange(NS)[None, :] == p // NQ
    cst[:, C_ONE] = 1.0
    lvl = np.zeros((P, len(LEVELS) + 1, P), np.float32)
    lvl[:, 0] = p == f
    for n, m in enumerate(LEVELS):
        lvl[:, n + 1] = (p // (2 * m) == f // (2 * m)) & (p % (2 * m) < m) & (f % (2 * m) >= m)
    keep = np.ones((P, T), np.float32)
    keep[:, 0:SEQ:P] = 0.0
    keep[:, SEQ::NQ] = 0.0
    return cst, lvl, keep


class Order:

    def __init__(self, eng, sem):
        self.eng, self.sem, self.n, self.it, self.per = eng, sem, 0, 0, 0

    def then(self, ins):
        ins.then_inc(self.sem, 1)
        self.n += 1
        self.eng.wait_ge(self.sem, self.it * self.per + self.n)

    def enter(self, it, per):
        self.it, self.per, self.start = it, per, self.n

    def leave(self, turns):
        assert self.n - self.start == self.per, (self.n - self.start, self.per)
        self.n += self.per * (turns - 1)
        self.it = self.per = 0


def build(nc, a, o, stop=99):
    ctx = ExitStack()
    with ctx:
        def sb(name, shape, dt=F32, where=ctx):
            return where.enter_context(nc.sbuf_tensor("sbuf_" + name, shape, dt))

        def sem(name):
            return ctx.enter_context(nc.semaphore(name))

        PS = ctx.enter_context(nc.psum_tensor("PS", [P, 8, 512], F32))
        cst = sb("cst", [P, C_END])
        lvl = sb("lvl", [P, len(LEVELS) + 1, P], U8)
        ident = cst[:, C_ID:C_ID + P]
        h_hi = sb("h_hi", [P, KB, T], F32R)
        h_lo = sb("h_lo", [P, KB, T], F32R)
        raw = [sb(f"raw{i}", [P, 1024]) for i in range(RAWS)]
        w_hi = [sb(f"w_hi{i}", [P, 1024], F32R) for i in range(SLOTS)]
        w_lo = [sb(f"w_lo{i}", [P, 1024], F32R) for i in range(SLOTS)]

        half = sb("half", [P, NT])

        with ExitStack() as heads:
            g_N = [sb(f"g_N{i}", [P, T], where=heads) for i in range(4)]
            with ExitStack() as ph:
                s_qN = sb("s_qN", [P, T], where=ph)
                s_kN = sb("s_kN", [P, T], where=ph)
                s_vN = sb("s_vN", [P, T], where=ph)
                s_out = sb("s_out", [P, NT, P], where=ph)
                s_qT = sb("s_qT", [P, T], where=ph)
                s_kT = sb("s_kT", [P, T], where=ph)
                s_k = sb("s_k", [P, NT, P], where=ph)
                s_v = sb("s_v", [P, NT, P], where=ph)
                s_E = sb("s_E", [P, 6, 512], where=ph)
                s_aT = sb("s_aT", [P, 4, 512], where=ph)
                s_sum = sb("s_sum", [P, 1], where=ph)
                s_cK = sb("s_cK", [P, 8, P], where=ph)
                s_cV = sb("s_cV", [P, 8, P], where=ph)
                s_KT = sb("s_KT", [P, 4, PAST + NQ], where=ph)
                s_QB = sb("s_QB", [P, 640], where=ph)
                s_own = sb("s_own", [P, P], where=ph)
                s_oT = sb("s_oT", [P, P], where=ph)
            with ExitStack() as ph:
                g_out = sb("g_out", [P, NT, P], where=ph)
                g_qT = sb("g_qT", [P, T], where=ph)
                g_kT = sb("g_kT", [P, T], where=ph)
                g_cum = sb("g_cum", [P, T], where=ph)
                g_D = sb("g_D", [P, T], where=ph)
                g_QL = sb("g_QL", [P, T], where=ph)
                g_KL = sb("g_KL", [P, T], where=ph)
                g_I = sb("g_I", [P, NT, P], where=ph)
                g_G = sb("g_G", [P, NT, P], where=ph)
                g_A = sb("g_A", [P, NT, P], where=ph)
                g_S = sb("g_S", [P, NT - 1, P], where=ph)
                g_S0 = sb("g_S0", [P, NS, P], where=ph)
                g_keep = sb("g_keep", [P, T], where=ph)
                g_gain = sb("g_gain", [P, HGW], where=ph)
                g_word = sb("g_word", [P, 32], where=ph)
                g_el = sb("g_el", [P, 16], where=ph)
                g_st = sb("g_st", [P, 2, NT], where=ph)
        with ExitStack() as ph0:
            X = sb("X", [P, NT, D], where=ph0)
            gain = sb("gain", [P, D], where=ph0)
            xn = sb("xn", [P, 2, D], where=ph0)
            st = sb("st", [P, 3, NT], where=ph0)
            with ExitStack() as ph:
                c_q = sb("c_q", [P, MEM_HEADS, T], where=ph)
                c_kT = sb("c_kT", [P, MEM_HEADS, NMEM], where=ph)
                c_v = sb("c_v", [P, 2, MEMW], where=ph)
                c_KT = sb("c_KT", [P, 4, NMEM], where=ph)
                c_V1 = sb("c_V1", [P, 8, P], where=ph)
                c_QB = sb("c_QB", [P, T], where=ph)
                c_w = sb("c_w", [P, 2, 2 * NMEM], where=ph)
                c_st = sb("c_st", [P, 4, MEM_HEADS * NT], where=ph)
            with ExitStack() as ph:
                u_hi = sb("u_hi", [P, FB, T], F32R, where=ph)
                u_lo = sb("u_lo", [P, FB, T], F32R, where=ph)
                f_r = sb("f_r", [P, T], where=ph)
                f_s = xn[:].rearrange("p a b -> p (a b)")[:, 0:T]

        landed = [sem(f"landed{i}") for i in range(RAWS)]
        cut_hi = [sem(f"cut_hi{i}") for i in range(RAWS)]
        cut_lo = [sem(f"cut_lo{i}") for i in range(RAWS)]
        slot_free = [sem(f"slot_free{i}") for i in range(SLOTS)]

        def unit_sb(p, s):
            return p, (2 * p + s // 2 if s % 2 == 0 else p)

        def unit(c, s):
            return c + (PAIRS if s < 3 else 0), 2 * c + s // 2 + (2 * PAIRS if s % 2 == 0 else PAIRS)

        R_HG = 0
        R_OUT = HG_HEADS
        R_MEM = R_OUT + 2
        R_MQ = R_MEM + 2
        R_MO = R_MQ + 1
        R_FF = R_MO + 1

        def cut_hi_unit(act, use, s):
            k, n = use
            act.wait_ge(landed[s % 2], n * 16 + 16)
            act.wait_ge(slot_free[s], k + 1)
            act.activation(w_hi[s][:], raw[s % 2][:], ACT.Copy).then_inc(cut_hi[s % 2], 1)

        def cut_lo_unit(dve, use, s):
            k, n = use
            dve.wait_ge(landed[s % 2], n * 16 + 16)
            dve.wait_ge(slot_free[s], k + 1)
            dve.wait_ge(cut_hi[s % 2], n + 1)
            dve.tensor_tensor(w_lo[s][:], raw[s % 2][:], w_hi[s][:].bitcast(F32),
                              ALU.subtract).then_inc(cut_lo[s % 2], 1)

        def wait_unit(pe, use, s):
            k, n = use
            pe.wait_ge(cut_hi[s % 2], n + 1)
            pe.wait_ge(cut_lo[s % 2], n + 1)

        bar = sem("bar")
        ENGINES = 4

        def barrier(eng, n, joins=True):
            if joins:
                eng.drain().then_inc(bar, 1)
            eng.wait_ge(bar, ENGINES * n)

        def settle(eng):
            eng.wait_ge(ld("cst"), 32)

        io = {}

        def ld(name):
            if name not in io:
                io[name] = sem("ld_" + name)
            return io[name]

        N = {x: sem("norm_" + x) for x in ("sq", "ms", "rs", "xn", "tr", "hi", "lo", "out")}
        norm_tiles = [0]

        class Norm:
            def __init__(self, tag, tiles, width, src, at=0, final=False, loads=None, load_at=16):
                self.tag, self.tiles, self.width, self.src, self.at, self.final = tag, tiles, width, src, at, final
                self.loads, self.load_at = loads, load_at
                self.base, norm_tiles[0] = norm_tiles[0], norm_tiles[0] + tiles

        def norm_act(act, n):
            def square(t):
                if n.loads:
                    act.wait_ge(n.loads[t], n.load_at)
                if n.final:
                    if t >= 2:
                        act.wait_ge(N["out"], 16 * (t - 1))
                elif t >= 2:
                    act.wait_ge(N["tr"], 2 * (n.base + t - 1))
                if t >= 2:
                    act.wait_ge(N["xn"], n.base + t - 1)
                act.activation(xn[:, t % 2, 0:n.width], n.src(t)[:, 0:n.width], ACT.Square,
                               accum_out=st[:, 0, t:t + 1]).then_inc(N["sq"], 1)

            square(0)
            for t in range(n.tiles):
                if t + 1 < n.tiles:
                    square(t + 1)
                if not n.final:
                    for half_ in range(2):
                        act.wait_ge(N["tr"], 2 * (n.base + t) + half_ + 1)
                        act.activation(h_hi[:, 4 * half_:4 * half_ + 4, n.at + t * P:n.at + (t + 1) * P],
                                       PS[:, 2 * (t % 2) + half_, :].rearrange("p (k c) -> p k c", k=4),
                                       ACT.Copy).then_inc(N["hi"], 1)

        def norm_dve(dve, n):
            def scale(t):
                dve.wait_ge(N["sq"], n.base + t + 1)
                dve.tensor_scalar(st[:, 1, t:t + 1], st[:, 0, t:t + 1], 1.0 / n.width, EPS, ALU.mult, ALU.add)\
                   .then_inc(N["ms"], 1)

            def rows(t):
                if n.loads:
                    dve.wait_ge(n.loads[t], n.load_at)
                dve.wait_ge(N["rs"], n.base + t + 1)
                dve.wait_ge(ld("gain"), 16 * n.gain_at)
                dve.scalar_tensor_tensor(xn[:, t % 2, 0:n.width], n.src(t)[:, 0:n.width], st[:, 2, t:t + 1],
                                         gain[:, 0:n.width], ALU.mult, ALU.mult).then_inc(N["xn"], 1)

            scale(0)
            rows(0)
            for t in range(n.tiles):
                if t + 1 < n.tiles:
                    scale(t + 1)
                    rows(t + 1)
                if not n.final:
                    for half_ in range(2):
                        dve.wait_ge(N["hi"], 2 * (n.base + t) + half_ + 1)
                        cols = slice(n.at + t * P, n.at + (t + 1) * P)
                        dve.tensor_tensor(h_lo[:, 4 * half_:4 * half_ + 4, cols],
                                          PS[:, 2 * (t % 2) + half_, :].rearrange("p (k c) -> p k c", k=4),
                                          h_hi[:, 4 * half_:4 * half_ + 4, cols].bitcast(F32),
                                          ALU.subtract).then_inc(N["lo"], 1)

        def norm_pool(pool, n):
            for t in range(n.tiles):
                pool.wait_ge(N["ms"], n.base + t + 1)
                pool.tensor_tensor(st[:, 2, t:t + 1], st[:, 1, t:t + 1], half[:, 0:1], ALU.pow)\
                    .then_inc(N["rs"], 1)

        def norm_pe(pe, n):
            for t in range(n.tiles):
                pe.wait_ge(N["xn"], n.base + t + 1)
                for half_ in range(2):
                    if t >= 2:
                        pe.wait_ge(N["lo"], 2 * (n.base + t - 2) + half_ + 1)
                    if n.loads:
                        pe.wait_ge(n.loads[t], n.load_at)
                    for k in range(4):
                        kb = 4 * half_ + k
                        src = xn[:, t % 2, kb * P:(kb + 1) * P] if kb * P < n.width else \
                            n.src(t)[:, kb * P:(kb + 1) * P]
                        last = pe.transpose(PS[:, 2 * (t % 2) + half_, k * P:(k + 1) * P], src, ident)
                    last.then_inc(N["tr"], 1)

        def project(pe, s, bank, ntok=T, group=TG):
            for g in range(ntok // group):
                tok = slice(g * group, (g + 1) * group)
                out = PS[:, bank + g, 0:group]
                for kb in range(KB):
                    hi, lo = w_hi[s][:, kb * P:(kb + 1) * P], w_lo[s][:, kb * P:(kb + 1) * P]
                    pe.matmul(out, hi, h_hi[:, kb, tok], start=kb == 0, stop=False)
                    pe.matmul(out, hi, h_lo[:, kb, tok], start=False, stop=False)
                    last = pe.matmul(out, lo, h_hi[:, kb, tok], start=False, stop=kb == KB - 1)
            last.then_inc(slot_free[s], 1)

        grp = sem("grp")
        gev = sem("gev")

        def project_group(pe, s, use, g, index, bank, rotate, part=0, parts=1):
            if g == 0 and part == 0:
                wait_unit(pe, use, s)
            if part > 0:
                pass
            elif not isinstance(index, int) or 3 * index + g >= rotate:
                pe.wait_ge(gev, 3 * index + g - rotate + 1)
            tok = slice(g * TG, (g + 1) * TG)
            out = PS[:, bank, 0:TG]
            for kb in range(part * KB // parts, (part + 1) * KB // parts):
                hi, lo = w_hi[s][:, kb * P:(kb + 1) * P], w_lo[s][:, kb * P:(kb + 1) * P]
                pe.matmul(out, hi, h_hi[:, kb, tok], start=kb == 0, stop=False)
                pe.matmul(out, hi, h_lo[:, kb, tok], start=False, stop=False)
                last = pe.matmul(out, lo, h_hi[:, kb, tok], start=False, stop=kb == KB - 1)
            if part == parts - 1:
                last.then_inc(slot_free[s] if g == 2 else grp, 1)

        def copy_group(act, s, use, g, index, bank, dst, scale):
            if g == 2:
                projected(act, use, s)
            else:
                act.wait_ge(grp, 2 * index + g + 1)
            act.activation(dst[:, g * TG:(g + 1) * TG], PS[:, bank, 0:TG], ACT.Copy, scale=scale).then_inc(gev, 1)

        def projected(eng, use, s):
            eng.wait_ge(slot_free[s], use[0] + 2)

        def bank3(bank):
            return PS[:, bank:bank + 3, 0:TG]

        def as3(x):
            return x.rearrange("p (g c) -> p g c", g=3)

        sb_q, sb_kT = sem("sb_q"), sem("sb_kT")
        sb_tr = sem("sb_tr")
        sb_k, sb_v = sem("sb_k"), sem("sb_v")
        sb_st = sem("sb_st")
        sb_z = sem("sb_z")
        sb_abs, sb_ex, sb_ln = sem("sb_abs"), sem("sb_ex"), sem("sb_ln")
        sb_arg = sem("sb_arg")
        sb_a = sem("sb_a")
        sb_tc, sb_te = sem("sb_tc"), sem("sb_te")
        sb_av = sem("sb_av")
        sb_dv = sem("sb_dv")
        sb_prep = sem("sb_prep")
        sb_own = sem("sb_own")
        sb_so = sem("sb_so")
        sb_soT = sem("sb_soT")
        sb_x = sem("sb_x")
        sb_cK, sb_cV = sem("sb_cK"), sem("sb_cV")
        sb_cKf = sem("sb_cKf")

        units_a = [(hh, i, first, min(4, i + 1 - first)) for hh in range(2) for i in range(SMP)
                   for first in reversed(range(0, i + 1, 4))]
        UA = len(units_a)
        U = UA + 2
        UK = UA - 4
        chunks = []
        for u in range(U):
            chunks.append(("a", u) + units_a[u][2:] if u < UA else ("s", u, 0, 3))
            if u - UK in (0, 1):
                chunks += [("K", u - UK, 0, 4), ("K", u - UK, 4, 4)]
        NC = len(chunks)
        of_unit = {u: next(c for c, x in enumerate(chunks) if x[0] in "as" and x[1] == u) for u in range(U)}
        of_K = {g: [c for c, x in enumerate(chunks) if x[0] == "K" and x[1] == g] for g in range(2)}
        ZB = 4
        EB = 6

        def keys_of(u):
            return units_a[u][3] * P if u < UA else PAST + NQ

        def diagonal(u):
            return u >= UA or units_a[u][2] + units_a[u][3] == units_a[u][1] + 1

        def zbank_sb(u):
            return PS[:, u % ZB, 0:keys_of(u)]

        def weights_of(u):
            return s_E[:, u % EB, 0:keys_of(u)]

        def qb_blocks(x):
            return x.rearrange("p (s c) -> p s c", c=160)

        def next_parts(last_pair):
            groups, parts = (12, 2) if last_pair else (9, 3)
            at = {}
            for n in range(groups * parts):
                at.setdefault(min(n, U - 1), []).append((n // parts // 3, n // parts % 3, n % parts, parts))
            return at

        def next_use(p, s):
            return unit_sb(p + 1, s) if s < 3 else unit(0, s)

        def cuts(p, last_pair):
            if last_pair:
                return {1: [(next_use(p, 2), 2)], 3: [(unit(0, 3), 3)], 6: [(unit(1, 0), 0)], 12: [(unit(1, 1), 1)],
                        19: [(unit(1, 2), 2)]}
            return {1: [(unit_sb(p + 1, 2), 2)], 9: [(unit_sb(p + 2, 0), 0)], 18: [(unit_sb(p + 2, 1), 1)]}

        def sb_pe(pe):
            def body(p, last_pair):
                for c in range(6):
                    if c == 0:
                        pe.wait_ge(gev, 9 * p + 9)
                    if c in (2, 3, 4):
                        pe.wait_ge(sb_k, p * 3 + c - 1)
                    if c == 5:
                        pe.wait_ge(sb_v, p * 3 + 1)
                    src = s_kN if c < 3 else s_vN
                    for n, t in enumerate(range(4 * (c % 3), min(4 * (c % 3) + 4, NT))):
                        last = pe.transpose(PS[:, 4 + c % 2, n * P:(n + 1) * P], src[:, t * P:(t + 1) * P], ident)
                    last.then_inc(sb_tr, 1)

                def z(u):
                    if u >= ZB:
                        pe.wait_ge(sb_arg, p * U + u - ZB + 1)
                    if u < UA:
                        hh, i, first, n = units_a[u]
                        rows = slice(HD * hh, HD * hh + HD)
                        last = pe.matmul(zbank_sb(u), s_qT[rows, i * P:(i + 1) * P],
                                         s_kT[rows, first * P:(first + n) * P], start=True, stop=True)
                    else:
                        for s in range(4):
                            last = pe.matmul(zbank_sb(u), s_QB[:, s * P:(s + 1) * P], s_KT[:, s, :],
                                             start=s == 0, stop=s == 3)
                    last.then_inc(sb_z, 1)

                def transposes(u):
                    pe.wait_ge(sb_a, p * U + u + 1)
                    c = of_unit[u]
                    if c >= 2:
                        pe.wait_ge(sb_te, p * NC + c - 1)
                    elif c == 0:
                        pe.wait_ge(sb_v, p * 3 + 3)
                    for j in range(chunks[c][3]):
                        if u >= UA and j == 2:
                            pe.wait_ge(sb_own, p * 2 + u - UA + 1)
                            src = s_own[:]
                        else:
                            src = s_E[:, u % EB, j * P:(j + 1) * P]
                        last = pe.transpose(PS[:, 4 + c % 2, j * P:(j + 1) * P], src, ident)
                    last.then_inc(sb_tc, 1)

                def cached_keys(g):
                    pe.wait_ge(sb_cK, p * 32 + 16 * g + 16)
                    for c in of_K[g]:
                        _, _, first, n = chunks[c]
                        pe.wait_ge(sb_te, p * NC + c - 1)
                        for j in range(n):
                            last = pe.transpose(PS[:, 4 + c % 2, j * P:(j + 1) * P], s_cK[:, first + j, :], ident)
                        last.then_inc(sb_tc, 1)
                    pe.wait_ge(sb_te, p * NC + of_K[g][-1] + 1)
                    pe.wait_ge(sb_prep, p * 2 + g + 1)

                def av(u):
                    pe.wait_ge(sb_te, p * NC + of_unit[u] + 1)
                    w = s_aT[:, u % 4, :]
                    if u < UA:
                        hh, i, first, n = units_a[u]
                        if u == UA // 2:
                            pe.wait_ge(sb_x, p * 3 + 1)
                        for j in range(n):
                            last = pe.matmul(PS[:, 6, i * HD:(i + 1) * HD], w[:, j * P:(j + 1) * P],
                                             s_v[:, first + j, hh * HD:(hh + 1) * HD],
                                             start=diagonal(u) and j == 0, stop=first == 0 and j == n - 1)
                    else:
                        g = u - UA
                        if g == 0:
                            pe.wait_ge(sb_x, p * 3 + 2)
                        pe.wait_ge(sb_cV, p * 32 + 16 * g + 16)
                        o_ = PS[:, 6, g * P:(g + 1) * P]
                        pe.matmul(o_, s_v[:, SMP, :], w[:, 2 * P:3 * P], start=True, stop=False,
                                  skip_group_check=True)
                        for s in range(4):
                            for kt in range(2):
                                last = pe.matmul(o_[:, s * 32:(s + 1) * 32], s_cV[:, 2 * s + kt, :],
                                                 w[:, kt * P + s * 32:kt * P + (s + 1) * 32],
                                                 start=False, stop=kt == 1, skip_group_check=True)
                    last.then_inc(sb_av, 1)

                pe.wait_ge(sb_q, p + 1)
                pe.wait_ge(sb_kT, p + 1)
                for u in range(ZB):
                    z(u)
                for u in range(U):
                    if u + ZB < UA:
                        z(u + ZB)
                    transposes(u)
                    if UA <= u + ZB < U:
                        cached_keys(u - UK)
                        z(u + ZB)
                    for s, g, part, parts in next_parts(last_pair).get(u, ()):
                        project_group(pe, s, next_use(p, s), g, 3 * p + 3 + s, 7, 1, part, parts)
                    if u:
                        av(u - 1)
                av(U - 1)
                pe.wait_ge(sb_so, p * 2 + 2)
                pe.transpose(PS[:, 4, 0:P], s_oT[:], ident).then_inc(sb_soT, 1)
                pe.wait_ge(sb_x, p * 3 + 3)

            for s in range(3):
                for g in range(3):
                    project_group(pe, s, unit_sb(0, s), g, s, 4 + (3 * s + g) % 4, 4)
            with pe.Fori(0, PAIRS - 1) as p:
                body(p, False)
            body(PAIRS - 1, True)

        def sb_act(act):
            def body(p, last_pair):
                def copy_next(u):
                    for s, g, part, parts in next_parts(last_pair).get(u - 1, ()):
                        if part < parts - 1:
                            continue
                        dst = g_N[s] if last_pair else (s_qN, s_kN, s_vN)[s]
                        copy_group(act, s, next_use(p, s), g, 3 * p + 3 + s, 7, dst, q_scale(s, last_pair))

                act.wait_ge(gev, 9 * p + 9)
                act.activation(s_kT[:], s_kN[:], ACT.Copy).then_inc(sb_kT, 1)
                for c in range(3, 6):
                    act.wait_ge(sb_tr, p * 6 + c + 1)
                    t0, t1 = 4 * (c - 3), min(4 * (c - 3) + 4, NT)
                    act.activation(s_v[:, t0:t1, :].rearrange("p t c -> p (t c)"), PS[:, 4 + c % 2, 0:(t1 - t0) * P],
                                   ACT.Copy).then_inc(sb_v, 1)

                def explog(u):
                    e = weights_of(u)
                    act.wait_ge(sb_z, p * U + u + 1)
                    if u >= EB:
                        act.wait_ge(sb_tc, p * NC + of_unit[u - EB] + 1)
                    act.activation(e, zbank_sb(u), ACT.Abs).then_inc(sb_abs, 1)
                    act.wait_ge(sb_abs, p * U + u + 1)
                    act.activation(e, e, ACT.Exp, scale=-1.0).then_inc(sb_ex, 1)
                    act.wait_ge(sb_ex, p * U + u + 1)
                    act.activation(e, e, ACT.Ln, bias=1.0).then_inc(sb_ln, 1)

                def weights(u):
                    e = weights_of(u)
                    act.wait_ge(sb_arg, p * U + u + 1)
                    act.activation(e, e, ACT.Exp).then_inc(sb_a, 1)

                def copy_out(u):
                    c = of_unit[u]
                    act.wait_ge(sb_tc, p * NC + c + 1)
                    if u >= 4:
                        act.wait_ge(sb_av, p * U + u - 3)
                    n = chunks[c][3]
                    act.activation(s_aT[:, u % 4, 0:n * P], PS[:, 4 + c % 2, 0:n * P], ACT.Copy).then_inc(sb_te, 1)

                def copy_keys(g):
                    for c in of_K[g]:
                        act.wait_ge(sb_tc, p * NC + c + 1)
                        if g == 1 and c == of_K[1][0]:
                            act.wait_ge(sb_z, p * U + UA + 1)
                        s0 = chunks[c][2] // 2
                        act.activation(s_KT[:, s0:s0 + 2, 0:PAST],
                                       PS[:, 4 + c % 2, :].rearrange("p (s k) -> p s k", s=2),
                                       ACT.Copy).then_inc(sb_te, 1)

                explog(0)
                explog(1)
                for u in range(U):
                    if u + 2 < U:
                        explog(u + 2)
                    if u:
                        copy_out(u - 1)
                    if u - 1 - UK in (0, 1):
                        copy_keys(u - 1 - UK)
                    weights(u)
                    copy_next(u)
                    for use, s in cuts(p, last_pair).get(u, ()):
                        cut_hi_unit(act, use, s)
                copy_out(U - 1)
                copy_next(U)

            for s in range(3):
                for g in range(3):
                    copy_group(act, s, unit_sb(0, s), g, s, 4 + (3 * s + g) % 4, (s_qN, s_kN, s_vN)[s], q_scale(s, False))
            for s in range(2):
                cut_hi_unit(act, unit_sb(1, s), s)
            with act.Fori(0, PAIRS - 1) as p:
                body(p, False)
            body(PAIRS - 1, True)

        def q_scale(s, hgrn):
            return (P if hgrn else HD) ** -0.5 if s == 0 else 1.0

        SB_DV = 102

        def sb_dve(dve):
            od = Order(dve, sb_dv)
            od.then(dve.memset(s_QB[:], 0.0))
            for s in range(2):
                cut_lo_unit(dve, unit_sb(1, s), s)

            def body(p, last_pair):
                dve.wait_ge(gev, 9 * p + 9)
                dve.tensor_copy(s_qT[:], s_qN[:]).then_inc(sb_q, 1)
                for c in range(3):
                    dve.wait_ge(sb_tr, p * 6 + c + 1)
                    t0, t1 = 4 * c, min(4 * c + 4, NT)
                    dve.tensor_copy(s_k[:, t0:t1, :].rearrange("p t c -> p (t c)"), PS[:, 4 + c % 2, 0:(t1 - t0) * P])\
                       .then_inc(sb_k, 1)

                def exponent(u):
                    n, e, z = keys_of(u), weights_of(u), zbank_sb(u)
                    w = P if u < UA else NQ
                    tri, neg = (C_TRI, C_NEG) if u < UA else (C_TRI16, C_NEG16)
                    dve.wait_ge(sb_ln, p * U + u + 1)
                    od.then(dve.scalar_tensor_tensor(e, z, 0.0, e, ALU.max, ALU.add))
                    if diagonal(u):
                        od.then(dve.tensor_tensor(e[:, n - w:n], e[:, n - w:n], cst[:, tri:tri + w], ALU.mult))
                    od.then(dve.tensor_tensor_scan(e[:, ::-1], cst[:, C_ONE:C_ONE + 1].broadcast_to([P, n]),
                                                   e[:, ::-1], 0.0, ALU.mult, ALU.add))
                    if not diagonal(u):
                        dve.scalar_tensor_tensor(e, z, s_sum[:, 0:1], e, ALU.subtract, ALU.subtract).then_inc(sb_arg, 1)
                        return
                    if u < UA and units_a[u][2] > 0:
                        od.then(dve.tensor_copy(s_sum[:, 0:1], e[:, 0:1]))
                    od.then(dve.tensor_tensor(e, z, e, ALU.subtract))
                    dve.tensor_tensor(e[:, n - w:n], e[:, n - w:n], cst[:, neg:neg + w], ALU.add)\
                       .then_inc(sb_arg, 1)

                def sample_group(g):
                    if g == 1:
                        dve.wait_ge(sb_z, p * U + UA + 1)
                    for hh in range(2):
                        rows = slice(hh * HD, (hh + 1) * HD)
                        last = dve.tensor_copy(
                            qb_blocks(s_QB[rows, :])[:, :, hh * NQ:(hh + 1) * NQ],
                            s_qT[rows, SEQ + g * 64:SEQ + (g + 1) * 64].rearrange("p (s c) -> p s c", c=NQ))
                        od.then(last)
                    dve.tensor_copy(s_KT[:, :, PAST:PAST + NQ],
                                    s_kT[:, SEQ + g * 64:SEQ + (g + 1) * 64].rearrange("p (s c) -> p s c", c=NQ))\
                       .then_inc(sb_prep, 1)

                def own(g):
                    dve.wait_ge(sb_a, p * U + UA + 1 + g)
                    if g == 1:
                        dve.wait_ge(sb_tc, p * NC + of_unit[UA] + 1)
                    dve.tensor_tensor(s_own[:].rearrange("p (s c) -> p s c", c=NQ),
                                      s_E[:, (UA + g) % EB, PAST:PAST + NQ].unsqueeze(1).broadcast_to([P, NS, NQ]),
                                      cst[:, C_BLK + g * P:C_BLK + (g + 1) * P].rearrange("p (s c) -> p s c", c=NQ),
                                      ALU.mult).then_inc(sb_own, 1)

                def head_out(hh):
                    dve.wait_ge(sb_av, p * U + UA // 2 * (hh + 1))
                    if hh == 0:
                        dve.wait_ge(sb_st, p * 80 + 64)
                    dve.tensor_copy(s_out[:, 0:SMP, hh * HD:(hh + 1) * HD],
                                    PS[:, 6, :].rearrange("p (t c) -> p t c", c=HD)).then_inc(sb_x, 1)

                def sample_out(g):
                    dve.wait_ge(sb_av, p * U + U)
                    for hh in range(2):
                        rows = slice(hh * HD, (hh + 1) * HD)
                        ins = dve.tensor_copy(
                            s_oT[rows, g * 64:(g + 1) * 64].rearrange("p (s c) -> p s c", c=NQ),
                            PS[rows, 6, g * P:(g + 1) * P].rearrange("p (s c) -> p s c", c=32)
                            [:, :, hh * NQ:(hh + 1) * NQ])
                        if hh == 0:
                            od.then(ins)
                        else:
                            ins.then_inc(sb_so, 1)

                for u in range(U):
                    exponent(u)
                    if u == UA // 2 + 1:
                        head_out(0)
                    if u - UK in (0, 1):
                        sample_group(u - UK)
                    if u == UA:
                        own(0)
                        head_out(1)
                    if u == UA + 1:
                        own(1)
                        sample_out(0)
                        sample_out(1)
                    for use, s in cuts(p, last_pair).get(u, ()):
                        cut_lo_unit(dve, use, s)
                dve.wait_ge(sb_soT, p + 1)
                dve.tensor_copy(s_out[:, SMP, :], PS[:, 4, 0:P]).then_inc(sb_x, 1)
                dve.wait_ge(sb_st, p * 80 + 64)

            with dve.Fori(0, PAIRS - 1) as p:
                od.enter(p, SB_DV)
                body(p, False)
            od.leave(PAIRS - 1)
            body(PAIRS - 1, True)

        names = ("q tcap tln karg k cum tr i g gcap gln gsp gsig gate darg dexp ql lvl pred "
                 "ecum qe kdarg kdexp kd kdt qem im u s o sout oh ms rs x st s0 dv el").split()
        G = {n: sem("hg_" + n) for n in names}
        lchunks = []
        for n in range(len(LEVELS) + 1):
            tiles = NT if n == 0 or LEVELS[n - 1] < NQ else SMP
            lchunks += [(n, t, min(4, tiles - t)) for t in range(0, tiles, 4)]
        NL = len(lchunks)
        NLV = len(LEVELS)

        def lcols(n):
            return T if n == 0 or LEVELS[n - 1] < NQ else SEQ

        def hg_pe(pe):
            def body(h, last_head):
                groups = [] if last_head else [(s, g) for s in range(4) for g in range(3)]

                def fill(n=1):
                    for _ in range(min(n, len(groups))):
                        s, g = groups.pop(0)
                        project_group(pe, s, unit(h + 1, s), g, 3 * PAIRS + 4 * h + 4 + s, 7, 1)

                pe.wait_ge(gev, 9 * PAIRS + 12 * h + 12)
                for c in range(6):
                    if c in (2, 3, 4):
                        pe.wait_ge(G["i"], h * 3 + c - 1)
                    if c == 5:
                        pe.wait_ge(G["g"], h * 3 + 1)
                    src = g_N[2] if c < 3 else g_N[3]
                    for n, t in enumerate(range(4 * (c % 3), min(4 * (c % 3) + 4, NT))):
                        last = pe.transpose(PS[:, 4 + c % 2, n * P:(n + 1) * P], src[:, t * P:(t + 1) * P], ident)
                    last.then_inc(G["tr"], 1)
                pe.wait_ge(G["q"], h + 1)
                pe.wait_ge(G["k"], h + 1)
                for c, (n, t0, nt) in enumerate(lchunks):
                    if t0 == 0 and n > 0:
                        fill()
                    if t0 == 0 and n > 0:
                        pe.wait_ge(G["ql"], h * NLV + n)
                    if c >= 4:
                        pe.wait_ge(G["pred"], h * NL + c - 3)
                    ql, kl = (g_qT, g_kT) if n == 0 else (g_QL, g_KL)
                    for j in range(nt):
                        cols = slice((t0 + j) * P, (t0 + j + 1) * P)
                        last = pe.matmul(PS[:, c % 4, j * P:(j + 1) * P], kl[:, cols], ql[:, cols],
                                         start=True, stop=True)
                    last.then_inc(G["lvl"], 1)
                fill(2)
                pe.wait_ge(G["kd"], h + 1)
                pe.wait_ge(G["g"], h * 3 + 3)
                for c in range(3):
                    if c == 2:
                        pe.wait_ge(G["kdt"], h * 3 + 1)
                    for n, t in enumerate(range(4 * c, min(4 * c + 4, NT))):
                        last = pe.transpose(PS[:, 4 + c % 2, n * P:(n + 1) * P], g_kT[:, t * P:(t + 1) * P], ident)
                    last.then_inc(G["tr"], 1)
                fill(1)
                pe.wait_ge(G["kdt"], h * 3 + 3)
                pe.wait_ge(G["pred"], h * NL + NL)
                for t in range(SMP):
                    last = pe.matmul(PS[:, t // 4, (t % 4) * P:(t % 4 + 1) * P], g_QL[:, t * P:(t + 1) * P],
                                     g_I[:, t, :], start=True, stop=True)
                last.then_inc(G["u"], 1)
                pe.wait_ge(G["im"], h + 1)
                for b in range(2):
                    last = pe.matmul(PS[:, 2 + b, :], g_QL[:, SEQ:T], g_D[:, 512 * b:512 * (b + 1)],
                                     start=True, stop=True)
                last.then_inc(G["u"], 1)
                fill(2)
                pe.wait_ge(G["qe"], h + 1)
                for t in range(SMP):
                    out = PS[:, 4 + t // 4, (t % 4) * P:(t % 4 + 1) * P]
                    last = pe.matmul(out, g_A[:, t, :], g_I[:, t, :], start=True, stop=t == 0)
                    if t > 0:
                        pe.wait_ge(G["s"], h * SMP + t)
                        last = pe.matmul(out, g_qT[:, t * P:(t + 1) * P], g_S[:, t - 1, :], start=False, stop=True)
                last.then_inc(G["o"], 1)
                pe.wait_ge(G["qem"], h + 1)
                pe.wait_ge(G["s0"], h * 16 + 16)
                out = PS[:, 6, 0:P]
                pe.matmul(out, g_A[:, SMP, :], g_I[:, SMP, :], start=True, stop=False)
                for s in range(NS):
                    last = pe.matmul(out, g_KL[:, s * P:(s + 1) * P], g_S0[:, s, :], start=False, stop=s == NS - 1)
                last.then_inc(G["o"], 1)
                pe.wait_ge(G["oh"], h * 2 + 2)
                pe.wait_ge(G["sout"], h + 1)

            with pe.Fori(0, HG_HEADS - 1) as h:
                body(h, False)
            body(HG_HEADS - 1, True)

        def hg_act(act):
            def step(out, in_, f, s, **kw):
                act.activation(out, in_, f, **kw).then_inc(G[s], 1)

            def body(h, last_head):
                groups = [] if last_head else [(s, g) for s in range(4) for g in range(3)]

                def fill(n=1):
                    for _ in range(min(n, len(groups))):
                        s, g = groups.pop(0)
                        copy_group(act, s, unit(h + 1, s), g, 3 * PAIRS + 4 * h + 4 + s, 7, g_N[s], q_scale(s, True))

                for c in range(3):
                    act.wait_ge(G["tr"], h * 9 + c + 1)
                    t0, t1 = 4 * c, min(4 * c + 4, NT)
                    step(g_I[:, t0:t1, :].rearrange("p t c -> p (t c)"), PS[:, 4 + c % 2, 0:(t1 - t0) * P],
                         ACT.Copy, "i")
                act.wait_ge(G["tcap"], h + 1)
                step(g_D[:], g_D[:], ACT.Exp, "tln", scale=-1.0)
                act.wait_ge(G["tln"], h * 2 + 1)
                step(g_D[:], g_D[:], ACT.Ln, "tln", bias=1.0)
                act.wait_ge(G["karg"], h + 1)
                step(g_kT[:], g_kT[:], ACT.Exp, "k")
                act.wait_ge(G["gcap"], h + 1)
                step(g_D[:], g_D[:], ACT.Exp, "gln", scale=-1.0)
                act.wait_ge(G["gln"], h * 2 + 1)
                step(g_D[:], g_D[:], ACT.Ln, "gln", bias=1.0)
                act.wait_ge(G["gsp"], h + 1)
                step(g_D[:], g_D[:], ACT.Exp, "gsig", scale=-1.0)
                for n in range(1, NLV + 1):
                    act.wait_ge(G["darg"], h * NLV + n)
                    step(g_D[:, 0:lcols(n)], g_D[:, 0:lcols(n)], ACT.Exp, "dexp")
                    fill()
                    if n == 1:
                        cut_hi_unit(act, unit(h + 1, 3), 3)
                    if n in (5, 7) and not last_head:
                        cut_hi_unit(act, unit(h + 2, (n - 5) // 2), (n - 5) // 2)
                act.wait_ge(G["ql"], h * NLV + NLV)
                step(g_D[:], g_cum[:], ACT.Exp, "ecum")
                fill(2)
                act.wait_ge(G["kdarg"], h + 1)
                step(g_D[:], g_D[:], ACT.Exp, "kdexp")
                for c in range(3):
                    act.wait_ge(G["tr"], h * 9 + 7 + c)
                    t0, t1 = 4 * c, min(4 * c + 4, NT)
                    step(g_QL[:, t0 * P:t1 * P], PS[:, 4 + c % 2, 0:(t1 - t0) * P], ACT.Copy, "kdt")
                fill(3)
                act.wait_ge(G["o"], h * 2 + 1)
                act.wait_ge(G["u"], h * 2 + 2)
                step(g_D[:, 0:SEQ].rearrange("p (b c) -> p b c", b=2), PS[:, 4:6, :], ACT.Copy, "oh")
                act.wait_ge(G["o"], h * 2 + 2)
                step(g_D[:, SEQ:T], PS[:, 6, 0:P], ACT.Copy, "oh")
                if not last_head:
                    cut_hi_unit(act, unit(h + 2, 2), 2)

            with act.Fori(0, HG_HEADS - 1) as h:
                body(h, False)
            body(HG_HEADS - 1, True)

        HG_DV = 6

        def hg_dve(dve):
            od = Order(dve, G["dv"])
            od.then(dve.memset(g_A[:], 0.0))
            od.then(dve.memset(g_QL[:], 0.0))
            od.then(dve.memset(g_KL[:], 0.0))

            def halves(x, n):
                m = LEVELS[n - 1]
                return x[:, 0:lcols(n)].rearrange("p (b h m) -> p b h m", h=2, m=m)

            def body(h, last_head):
                z = g_N[1][:]
                dve.wait_ge(gev, 9 * PAIRS + 12 * h + 12)
                dve.tensor_scalar(g_D[:], z, -CAP, None, ALU.max).then_inc(G["tcap"], 1)
                dve.tensor_copy(g_qT[:], g_N[0][:]).then_inc(G["q"], 1)
                dve.wait_ge(G["tln"], h * 2 + 2)
                od.then(dve.scalar_tensor_tensor(g_cum[:], g_D[:], -1.0, z, ALU.mult, ALU.min))
                dve.tensor_tensor(g_kT[:], g_cum[:], z, ALU.subtract).then_inc(G["karg"], 1)
                dve.wait_ge(ld("keep"), 16)
                dve.tensor_tensor_scan(g_cum[:], g_keep[:], g_cum[:], 0.0, ALU.mult, ALU.add).then_inc(G["cum"], 1)
                for c in range(3):
                    dve.wait_ge(G["tr"], h * 9 + c + 4)
                    t0, t1 = 4 * c, min(4 * c + 4, NT)
                    dve.tensor_copy(g_G[:, t0:t1, :].rearrange("p t c -> p (t c)"),
                                    PS[:, 4 + (c + 1) % 2, 0:(t1 - t0) * P]).then_inc(G["g"], 1)
                flatG = g_G[:].rearrange("p t c -> p (t c)")
                dve.wait_ge(G["g"], h * 3 + 3)
                dve.wait_ge(G["karg"], h + 1)
                dve.tensor_scalar(g_D[:], flatG, -CAP, None, ALU.max).then_inc(G["gcap"], 1)
                dve.wait_ge(G["gln"], h * 2 + 2)
                dve.scalar_tensor_tensor(g_D[:], flatG, -1.0, g_D[:], ALU.mult, ALU.max).then_inc(G["gsp"], 1)
                dve.wait_ge(G["gsig"], h + 1)
                dve.tensor_tensor(flatG, flatG, g_D[:], ALU.mult).then_inc(G["gate"], 1)
                dve.wait_ge(G["gate"], h + 1)
                dve.wait_ge(G["cum"], h + 1)

                def distance(n):
                    c, d = halves(g_cum[:], n), halves(g_D[:], n)
                    m = LEVELS[n - 1]
                    ref = c[:, :, 0, m - 1:m].broadcast_to([P, lcols(n) // (2 * m), m])
                    od_ = dve.tensor_tensor(d[:, :, 1, :], c[:, :, 1, :], ref, ALU.subtract)
                    dve.tensor_tensor(d[:, :, 0, :], ref, c[:, :, 0, :], ALU.subtract).then_inc(G["darg"], 1)

                def factors(n):
                    dve.wait_ge(G["dexp"], h * NLV + n)
                    if n > 1:
                        last = max(c for c, x in enumerate(lchunks) if x[0] == n - 1)
                        dve.wait_ge(G["lvl"], h * NL + last + 1)
                    d, q, k = (halves(x[:], n) for x in (g_D, g_qT, g_kT))
                    if n == 1:
                        dve.wait_ge(G["k"], h + 1)
                        dve.wait_ge(G["q"], h + 1)
                        dve.wait_ge(G["tr"], h * 9 + 6)
                    dve.tensor_tensor(halves(g_QL[:], n)[:, :, 1, :], q[:, :, 1, :], d[:, :, 1, :], ALU.mult)
                    dve.tensor_tensor(halves(g_KL[:], n)[:, :, 0, :], k[:, :, 0, :], d[:, :, 0, :], ALU.mult)\
                       .then_inc(G["ql"], 1)

                def pick(n):
                    for c, (lv, t0, nt) in enumerate(lchunks):
                        if lv != n:
                            continue
                        before = [b for b in range(c) if lchunks[b][1] == t0]
                        dve.wait_ge(G["lvl"], h * NL + c + 1)
                        if n > 0:
                            dve.wait_ge(G["pred"], h * NL + before[-1] + 1)
                        dve.memset(g_word[:, c:c + 1], 0.0)
                        dve.copy_predicated(g_A[:, t0:t0 + nt, :], lvl[:, n, :].unsqueeze(1).broadcast_to([P, nt, P]),
                                            PS[:, c % 4, 0:nt * P].rearrange("p (t c) -> p t c", c=P))\
                           .then_inc(G["pred"], 1)

                distance(1)
                factors(1)
                pick(0)
                for n in range(1, NLV + 1):
                    if n < NLV:
                        dve.wait_ge(G["ql"], h * NLV + n)
                        distance(n + 1)
                    pick(n)
                    if n < NLV:
                        factors(n + 1)
                    if n == 1:
                        cut_lo_unit(dve, unit(h + 1, 3), 3)
                    if n in (5, 7) and not last_head:
                        cut_lo_unit(dve, unit(h + 2, (n - 5) // 2), (n - 5) // 2)
                dve.wait_ge(G["ecum"], h + 1)
                dve.tensor_copy(g_el[:, 0:8], g_D[:, 0:SEQ].rearrange("p (t c) -> p t c", c=P)[:, :, P - 1])
                dve.tensor_copy(g_el[:, 8:16], g_D[:, SEQ:T].rearrange("p (t c) -> p t c", c=NQ)[:, :, NQ - 1])\
                   .then_inc(G["el"], 1)
                last = max(c for c in range(NL))
                dve.wait_ge(G["lvl"], h * NL + last + 1)
                dve.tensor_tensor(g_qT[:], g_qT[:], g_D[:], ALU.mult).then_inc(G["qe"], 1)
                dve.wait_ge(G["qe"], h + 1)
                dve.wait_ge(G["el"], h + 1)
                for lo, hi, c in ((0, SEQ, P), (SEQ, T, NQ)):
                    x = g_cum[:, lo:hi].rearrange("p (t c) -> p t c", c=c)
                    ins = dve.tensor_tensor(g_D[:, lo:hi].rearrange("p (t c) -> p t c", c=c),
                                            x[:, :, c - 1:c].broadcast_to([P, (hi - lo) // c, c]), x, ALU.subtract)
                ins.then_inc(G["kdarg"], 1)
                od.then(dve.memset(g_KL[:], 0.0))
                dve.tensor_copy(g_KL[:].rearrange("p (s c) -> p s c", c=P + NQ)[:, :, 0:NQ],
                                g_qT[:, SEQ:T].rearrange("p (s c) -> p s c", c=NQ)).then_inc(G["qem"], 1)
                dve.wait_ge(G["kdexp"], h + 1)
                dve.tensor_tensor(g_kT[:], g_kT[:], g_D[:], ALU.mult).then_inc(G["kd"], 1)
                dve.wait_ge(G["kd"], h + 1)
                dve.tensor_tensor(g_D[:, 0:SEQ].rearrange("p (s c) -> p s c", c=P),
                                  g_I[:, SMP, :].unsqueeze(1).broadcast_to([P, NS, P]),
                                  cst[:, C_STR:C_STR + NS].unsqueeze(2).broadcast_to([P, NS, P]),
                                  ALU.mult).then_inc(G["im"], 1)
                dve.wait_ge(G["u"], h * 2 + 1)
                for t in range(SMP):
                    u = PS[:, t // 4, (t % 4) * P:(t % 4 + 1) * P]
                    if t == 0:
                        ins = dve.tensor_copy(g_S[:, 0, :], u)
                    else:
                        dve.wait_ge(G["s"], h * SMP + t)
                        ins = dve.scalar_tensor_tensor(g_S[:, t, :], g_S[:, t - 1, :], g_el[:, t:t + 1], u,
                                                       ALU.mult, ALU.add)
                    ins.then_inc(G["s"], 1)
                dve.wait_ge(G["u"], h * 2 + 2)
                dve.wait_ge(G["o"], h * 2 + 2)
                for s in range(NS):
                    ins = dve.scalar_tensor_tensor(g_S0[:, s, :], g_S0[:, s, :], g_el[:, 8 + s:9 + s],
                                                   PS[:, 2 + s // 4, (s % 4) * P:(s % 4 + 1) * P],
                                                   ALU.mult, ALU.add)
                ins.then_inc(G["sout"], 1)
                dve.wait_ge(G["oh"], h * 2 + 2)
                od.then(dve.tensor_tensor(g_cum[:], g_D[:], g_D[:], ALU.mult))
                od.then(dve.tensor_reduce(g_st[:, 0, :], g_cum[:].rearrange("p (t c) -> p t c", c=P), AX_X, ALU.add))
                dve.tensor_scalar(g_st[:, 0, :], g_st[:, 0, :], 1.0 / P, EPS, ALU.mult, ALU.add).then_inc(G["ms"], 1)
                flatG = g_G[:].rearrange("p t c -> p (t c)")
                od.then(dve.tensor_tensor(g_D[:], g_D[:], flatG, ALU.mult))
                dve.wait_ge(G["rs"], h + 1)
                oh = g_D[:].rearrange("p (t c) -> p t c", c=P)
                od.then(dve.tensor_tensor(oh, oh, g_st[:, 1, :].unsqueeze(2).broadcast_to([P, NT, P]), ALU.mult))
                dve.tensor_tensor(g_out[:], oh,
                                  g_gain[:, bass.ds(h * P, P)].unsqueeze(1).broadcast_to([P, NT, P]),
                                  ALU.mult).then_inc(G["x"], 1)
                dve.wait_ge(G["x"], h + 1)
                if not last_head:
                    cut_lo_unit(dve, unit(h + 2, 2), 2)
                dve.wait_ge(G["st"], h * 48 + 48)

            with dve.Fori(0, HG_HEADS - 1) as h:
                od.enter(h, HG_DV)
                body(h, False)
            od.leave(HG_HEADS - 1)
            body(HG_HEADS - 1, True)

        def hg_pool(pool):
            with pool.Fori(0, HG_HEADS) as h:
                pool.wait_ge(G["ms"], h + 1)
                pool.tensor_tensor(g_st[:, 1, :], g_st[:, 0, :], half[:], ALU.pow)\
                    .then_inc(G["rs"], 1)

        def add_out(tag):
            return sem(f"{tag}_y"), sem(f"{tag}_add")

        def out_pe(pe, sems, round0, op_hi, op_lo, nkb, per_half, banks=(0, 1)):
            y, add = sems
            n = 0
            for half_ in range(2):
                units = [(round0 + (half_ * per_half + j) // SLOTS, (half_ * per_half + j) % SLOTS)
                         for j in range(per_half)]
                for c, s in units:
                    wait_unit(pe, unit(c, s), s)
                for t in range(NT):
                    if n >= 2:
                        pe.wait_ge(add, n - 1)
                    out = PS[:, banks[n % 2], :]
                    tok = slice(t * P, (t + 1) * P)
                    for kb in range(nkb):
                        s = units[kb // 2][1]
                        cols = slice((kb % 2) * 512, (kb % 2 + 1) * 512)
                        pe.matmul(out, op_hi[:, kb, tok], w_hi[s][:, cols], start=kb == 0, stop=False)
                        pe.matmul(out, op_lo[:, kb, tok], w_hi[s][:, cols], start=False, stop=False)
                        last = pe.matmul(out, op_hi[:, kb, tok], w_lo[s][:, cols], start=False, stop=kb == nkb - 1)
                        if t == NT - 1 and kb % 2:
                            last.then_inc(slot_free[s], 1)
                    if t < NT - 1:
                        last.then_inc(y, 1)
                    n += 1

        def out_dve(dve, sems, round0, per_half, banks=(0, 1), between=None):
            y, add = sems
            n = 0
            for half_ in range(2):
                for t in range(NT):
                    if t < NT - 1:
                        dve.wait_ge(y, half_ * (NT - 1) + t + 1)
                    else:
                        end = half_ * per_half + per_half - 1
                        projected(dve, unit(round0 + end // SLOTS, end % SLOTS), end % SLOTS)
                    x = X[:, t, half_ * 512:(half_ + 1) * 512]
                    dve.tensor_tensor(x, PS[:, banks[n % 2], :], x, ALU.add).then_inc(add, 1)
                    n += 1
                if between:
                    between(half_)

        m_ev, m_tr, m_tev, m_st = (sem("m_" + x) for x in ("ev", "tr", "tev", "st"))
        mt_ = c_KT[:].rearrange("p s k -> p (s k)")

        def mem_pe(pe):
            for j in range(8):
                c, s = R_MEM + j // 4, j % 4
                wait_unit(pe, unit(c, s), s)
                if j >= 2:
                    pe.wait_ge(m_ev, j - 1)
                project(pe, s, j % 2, NMEM, NMEM)
            for j in range(8):
                pe.wait_ge(m_ev, j + 1)
                if j >= 2:
                    pe.wait_ge(m_tev, j - 1)
                src = c_kT[:, j, :] if j < 4 else mt_[:, (j - 4) * NMEM:(j - 3) * NMEM]
                for t in range(2):
                    last = pe.transpose(PS[:, 2 + j % 2, t * P:(t + 1) * P], src[:, t * P:(t + 1) * P], ident)
                last.then_inc(m_tr, 1)

        def mem_act(act):
            for j in range(8):
                projected(act, unit(R_MEM + j // 4, j % 4), j % 4)
                dst = c_kT[:, j, :] if j < 4 else mt_[:, (j - 4) * NMEM:(j - 3) * NMEM]
                act.activation(dst, PS[:, j % 2, 0:NMEM], ACT.Copy).then_inc(m_ev, 1)
                if j < 4:
                    cut_hi_unit(act, unit(R_MEM + 1, j), j)
                else:
                    cut_hi_unit(act, unit(R_MQ, j - 4), j - 4)

        def mem_dve(dve):
            for j in range(8):
                if j < 4:
                    cut_lo_unit(dve, unit(R_MEM + 1, j), j)
                else:
                    cut_lo_unit(dve, unit(R_MQ, j - 4), j - 4)
            for j in range(8):
                dve.wait_ge(m_tr, j + 1)
                dst = xn[:, 0, :].rearrange("p (t c) -> p t c", t=2) if j < 4 else c_v[:]
                dve.tensor_copy(dst[:, :, (j % 4) * P:(j % 4 + 1) * P],
                                PS[:, 2 + j % 2, 0:NMEM].rearrange("p (t c) -> p t c", t=2)).then_inc(m_tev, 1)

        c_ev = sem("c_ev")
        CN = {n: sem("c_" + n) for n in
              "z max nb ex rc p tr te av hi lo kt ke prep ko QB dv ldK ldV vfree".split()}
        units_c = [(hd, t, min(2, SMP - t) or 1) for hd in range(MEM_HEADS) for t in range(0, NT, 2)]
        UH = len(units_c) // MEM_HEADS
        NU = len(units_c)
        CZ = (0, 1, 6)

        def zbank(n, nt):
            return PS[:, CZ[n % 3], 0:nt * NMEM]

        def c_P(n):
            return c_w[:, n % 3, :] if n % 3 < 2 else cst[:, C_TRI:C_TRI + 2 * NMEM]

        def c_PT(n):
            return gain[:, (n % 2) * 2 * NMEM:(n % 2 + 1) * 2 * NMEM]

        def stat(i, n):
            hd, t, nt = units_c[n]
            return c_st[:, i, hd * NT + t:hd * NT + t + nt]

        def ogroup(n):
            hd, t, nt = units_c[n]
            return hd * 3 + t // 4 if t + nt in (4, SMP, NT) else None

        def mq_pe(pe):
            for j in range(4):
                wait_unit(pe, unit(R_MQ, j), j)
                if j >= 2:
                    pe.wait_ge(c_ev, j - 1)
                project(pe, j, 3 * (j % 2))

        def mq_act(act):
            for j in range(4):
                projected(act, unit(R_MQ, j), j)
                act.activation(as3(c_q[:, j, :]), bank3(3 * (j % 2)), ACT.Copy).then_inc(c_ev, 1)
                cut_hi_unit(act, unit(R_MO, j), j)

        def mq_dve(dve):
            for j in range(4):
                cut_lo_unit(dve, unit(R_MO, j), j)

        ogroups = [(hd, t0, min(4, NT - t0)) for hd in range(MEM_HEADS) for t0 in (0, 4, 8)]

        def cross_pe(pe):
            pe.wait_ge(c_ev, 4)

            def z(n):
                hd, t, nt = units_c[n]
                if n >= 3:
                    pe.wait_ge(CN["ex"], n - 2)
                if t < SMP:
                    for j in range(nt):
                        last = pe.matmul(zbank(n, nt)[:, j * NMEM:(j + 1) * NMEM],
                                         c_q[:, hd, (t + j) * P:(t + j + 1) * P], c_kT[:, hd, :],
                                         start=True, stop=True)
                    last.then_inc(CN["z"], 1)
                    return
                for g in range(2):
                    pe.wait_ge(CN["ldK"], 16 * (2 * hd + g) + 16)
                    for b in range(2):
                        kc = (2 * hd + g) * 2 + b
                        if kc >= 1:
                            pe.wait_ge(CN["ke"], kc)
                        for j in range(4):
                            last = pe.transpose(PS[:, 7, j * P:(j + 1) * P],
                                                xn[:, 0, :].rearrange("p (b c) -> p b c", c=P)[:, 4 * b + j, :], ident)
                        last.then_inc(CN["kt"], 1)
                    pe.wait_ge(CN["ke"], (2 * hd + g) * 2 + 2)
                    if g == 0:
                        pe.wait_ge(CN["QB"], hd + 1)
                    for s in range(4):
                        last = pe.matmul(zbank(n, 1), c_QB[:, (4 * g + s) * P:(4 * g + s + 1) * P],
                                         c_KT[:, s, :], start=g == 0 and s == 0, stop=g == 1 and s == 3)
                    if g == 0:
                        last.then_inc(CN["ko"], 1)
                last.then_inc(CN["z"], 1)

            def transposes(n):
                pe.wait_ge(CN["p"], n + 1)
                if n >= 2:
                    pe.wait_ge(CN["te"], n - 1)
                for j in range(2 * units_c[n][2]):
                    last = pe.transpose(PS[:, 2 + n % 2, j * P:(j + 1) * P], c_P(n)[:, j * P:(j + 1) * P], ident)
                last.then_inc(CN["tr"], 1)

            def av(n):
                hd, t, nt = units_c[n]
                grp = hd * 3 + t // 4
                if t % 4 == 0 and grp >= 2:
                    pe.wait_ge(CN["lo"], grp - 1)
                pe.wait_ge(CN["te"], n + 1)
                if t < SMP:
                    for j in range(nt):
                        out = PS[:, 4 + grp % 2, (t % 4 + j) * P:(t % 4 + j + 1) * P]
                        for kt in range(2):
                            last = pe.matmul(out, c_v[:, kt, hd * P:(hd + 1) * P],
                                             c_PT(n)[:, (2 * j + kt) * P:(2 * j + kt + 1) * P],
                                             start=kt == 0, stop=kt == 1)
                else:
                    out = PS[:, 4 + grp % 2, 0:P]
                    for g in range(2):
                        pe.wait_ge(CN["ldV"], 16 * (2 * hd + g) + 16)
                        V = xn[:, 1, :].rearrange("p (b c) -> p b c", c=P) if g == 0 else c_V1[:]
                        for s in range(4):
                            sc = slice((4 * g + s) * NQ, (4 * g + s + 1) * NQ)
                            for kt in range(2):
                                last = pe.matmul(out[:, sc], V[:, 2 * s + kt, :],
                                                 c_PT(n)[:, kt * P:(kt + 1) * P][:, sc],
                                                 start=kt == 0, stop=kt == 1)
                last.then_inc(CN["av"], 1)

            z(0)
            z(1)
            for n in range(NU):
                if n + 2 < NU:
                    z(n + 2)
                transposes(n)
                if n:
                    av(n - 1)
            av(NU - 1)

        def cross_act(act):
            def ex(n):
                act.wait_ge(CN["nb"], n + 1)
                if n >= 3:
                    act.wait_ge(CN["tr"], n - 2)
                nt = units_c[n][2]
                for j in range(nt):
                    cols = slice(j * NMEM, (j + 1) * NMEM)
                    ins = act.activation(c_P(n)[:, cols], zbank(n, nt)[:, cols], ACT.Exp,
                                         bias=stat(1, n)[:, j:j + 1], scale=P ** -0.5,
                                         accum_out=stat(2, n)[:, j:j + 1])
                ins.then_inc(CN["ex"], 1)

            def keys(n):
                hd = units_c[n][0]
                for kc in range(4):
                    k = hd * 4 + kc
                    act.wait_ge(CN["kt"], k + 1)
                    if kc == 0 and hd > 0:
                        act.wait_ge(CN["z"], n - UH + 1)
                    if kc == 2:
                        act.wait_ge(CN["ko"], hd + 1)
                    act.activation(c_KT[:, 2 * (kc % 2):2 * (kc % 2) + 2, :],
                                   PS[:, 7, :].rearrange("p (s k) -> p s k", s=2), ACT.Copy)\
                       .then_inc(CN["ke"], 1)

            def high(n):
                grp = ogroup(n)
                if grp is not None:
                    hd, t0, nt = ogroups[grp]
                    act.wait_ge(CN["av"], n + 1)
                    act.activation(h_hi[:, hd, t0 * P:(t0 + nt) * P], PS[:, 4 + grp % 2, 0:nt * P],
                                   ACT.Copy).then_inc(CN["hi"], 1)

            ex(0)
            ex(1)
            for n in range(NU):
                if n + 2 < NU:
                    if units_c[n + 2][1] == SMP:
                        keys(n + 2)
                    ex(n + 2)
                act.wait_ge(CN["tr"], n + 1)
                if n >= 2:
                    act.wait_ge(CN["av"], n - 1)
                w = 2 * P * units_c[n][2]
                act.activation(c_PT(n)[:, 0:w], PS[:, 2 + n % 2, 0:w], ACT.Copy).then_inc(CN["te"], 1)
                if n:
                    high(n - 1)
            high(NU - 1)

        def cross_dve(dve):
            dve.wait_ge(c_ev, 4)
            od = Order(dve, CN["dv"])
            od.then(dve.memset(c_QB[:], 0.0))

            def bias(n):
                hd, t, nt = units_c[n]
                if t == SMP:
                    if hd > 0:
                        dve.wait_ge(CN["z"], n - UH + 1)
                    dve.tensor_copy(c_QB[:].rearrange("p (s c) -> p s c", c=P + NQ)[:, :, 0:NQ],
                                    c_q[:, hd, SEQ:T].rearrange("p (s c) -> p s c", c=NQ)).then_inc(CN["QB"], 1)
                dve.wait_ge(CN["z"], n + 1)
                dve.reduce_max(stat(0, n), zbank(n, nt).rearrange("p (t c) -> p t c", t=nt), AX_X)\
                   .then_inc(CN["max"], 1)
                dve.wait_ge(CN["max"], n + 1)
                dve.tensor_scalar(stat(1, n), stat(0, n), -(P ** -0.5), None, ALU.mult).then_inc(CN["nb"], 1)

            def low(n):
                grp = ogroup(n)
                if grp is not None:
                    hd, t0, nt = ogroups[grp]
                    dve.wait_ge(CN["hi"], grp + 1)
                    dve.tensor_tensor(h_lo[:, hd, t0 * P:(t0 + nt) * P], PS[:, 4 + grp % 2, 0:nt * P],
                                      h_hi[:, hd, t0 * P:(t0 + nt) * P].bitcast(F32), ALU.subtract)\
                       .then_inc(CN["lo"], 1)

            bias(0)
            bias(1)
            for n in range(NU):
                if n + 2 < NU:
                    bias(n + 2)
                nt = units_c[n][2]
                dve.wait_ge(CN["ex"], n + 1)
                dve.reciprocal(stat(3, n), stat(2, n)).then_inc(CN["rc"], 1)
                dve.wait_ge(CN["rc"], n + 1)
                w = c_P(n)[:, 0:nt * NMEM].rearrange("p (t c) -> p t c", t=nt)
                dve.tensor_tensor(w, w, stat(3, n).unsqueeze(2).broadcast_to([P, nt, NMEM]), ALU.mult)\
                   .then_inc(CN["p"], 1)
                if n >= 2:
                    low(n - 2)
            low(NU - 2)
            low(NU - 1)

        f_rl, f_hi, f_sq, f_lo, f_y, f_add = (sem("f_" + x) for x in ("rl", "hi", "sq", "lo", "y", "add"))

        def ff_round(g, second):
            return R_FF + g * 2 + second

        def ff_loop(eng, body):
            with eng.Fori(0, FG - 1) as g:
                body(g, False)
            body(FG - 1, True)

        def ff_pe(pe):
            def body(g, last_turn):
                for b in range(FB):
                    wait_unit(pe, unit(ff_round(g, 0), b), b)
                    if b >= 2:
                        pe.wait_ge(f_rl, g * FB + b - 1)
                    project(pe, b, 3 * (b % 2))
                for half_ in range(2):
                    for s in (2 * half_, 2 * half_ + 1):
                        wait_unit(pe, unit(ff_round(g, 1), s), s)
                    for t in range(NT):
                        n = half_ * NT + t
                        if n >= 2:
                            pe.wait_ge(f_add, g * 2 * NT + n - 1)
                        for b in range(FB):
                            if n == 0:
                                pe.wait_ge(f_lo, g * FB + b + 1)
                            s = 2 * half_ + b // 2
                            cols = slice((b % 2) * 512, (b % 2 + 1) * 512)
                            tok = slice(t * P, (t + 1) * P)
                            out = PS[:, 6 + n % 2, :]
                            pe.matmul(out, u_hi[:, b, tok], w_hi[s][:, cols], start=b == 0, stop=False)
                            pe.matmul(out, u_lo[:, b, tok], w_hi[s][:, cols], start=False, stop=False)
                            last = pe.matmul(out, u_hi[:, b, tok], w_lo[s][:, cols], start=False, stop=b == FB - 1)
                            if t == NT - 1 and b % 2:
                                last.then_inc(slot_free[s], 1)
                        if t < NT - 1:
                            last.then_inc(f_y, 1)
                pe.wait_ge(f_add, g * 2 * NT + 2 * NT)

            ff_loop(pe, body)

        def ff_act(act):
            def body(g, last_turn):
                for b in range(FB):
                    projected(act, unit(ff_round(g, 0), b), b)
                    if b:
                        act.wait_ge(f_sq, g * FB + b)
                        act.wait_ge(f_hi, g * FB + b)
                    act.activation(as3(f_r[:]), bank3(3 * (b % 2)), ACT.Relu).then_inc(f_rl, 1)
                    act.wait_ge(f_rl, g * FB + b + 1)
                    act.activation(u_hi[:, b, :], f_r[:], ACT.Square).then_inc(f_hi, 1)
                    cut_hi_unit(act, unit(ff_round(g, 1), b), b)
                act.wait_ge(f_sq, g * FB + FB)
                if not last_turn:
                    for b in range(FB):
                        cut_hi_unit(act, unit(ff_round(g, 2), b), b)

            ff_loop(act, body)

        def ff_dve(dve):
            def body(g, last_turn):
                for b in range(FB):
                    dve.wait_ge(f_rl, g * FB + b + 1)
                    if b:
                        dve.wait_ge(f_lo, g * FB + b)
                    dve.tensor_tensor(f_s, f_r[:], f_r[:], ALU.mult).then_inc(f_sq, 1)
                    dve.wait_ge(f_sq, g * FB + b + 1)
                    dve.wait_ge(f_hi, g * FB + b + 1)
                    dve.tensor_tensor(u_lo[:, b, :], f_s, u_hi[:, b, :].bitcast(F32), ALU.subtract)\
                       .then_inc(f_lo, 1)
                    cut_lo_unit(dve, unit(ff_round(g, 1), b), b)
                dve.wait_ge(f_lo, g * FB + FB)
                for half_ in range(2):
                    for t in range(NT):
                        n = half_ * NT + t
                        if t < NT - 1:
                            dve.wait_ge(f_y, g * 2 * (NT - 1) + half_ * (NT - 1) + t + 1)
                        else:
                            projected(dve, unit(ff_round(g, 1), 2 * half_ + 1), 2 * half_ + 1)
                        x = X[:, t, half_ * 512:(half_ + 1) * 512]
                        dve.tensor_tensor(x, PS[:, 6 + n % 2, :], x, ALU.add).then_inc(f_add, 1)
                    if not last_turn:
                        for s in (2 * half_, 2 * half_ + 1):
                            cut_lo_unit(dve, unit(ff_round(g, 2), s), s)
                dve.wait_ge(f_add, g * 2 * NT + 2 * NT)

            ff_loop(dve, body)

        mix = nc.dram_tensor("mix", (T, D), F32).ap()
        mix_t = mix.rearrange("(t p) c -> p t c", p=P)
        xl = [sem(f"x_in{t}") for t in range(NT)]
        ml = [sem(f"mem_in{t}") for t in range(2)]
        wo_s, mo_s = add_out("wo"), add_out("mo")
        xrow = lambda t: X[:, t, :]
        mrow = lambda t: c_q[:, t, 0:D]
        n_mix = Norm("mix", NT, D, xrow, loads=xl)
        n_sb = Norm("sb", NT, SBW, xrow, loads=xl, load_at=32)
        n_mem = Norm("mem", 2, D, mrow, loads=ml)
        n_mq = Norm("mq", NT, D, xrow)
        n_ff = Norm("ff", NT, D, xrow)
        n_fin = Norm("fin", NT, D, xrow, final=True)
        for g_at, n in enumerate((n_mix, n_sb, n_mem, n_mq, n_ff, n_fin)):
            n.gain_at = g_at + 1
        B_MIX, B_SB, B_HG, B_MN, B_WO, B_MEM, B_MQN, B_CR, B_MO, B_FN, B_FF, B_FIN = range(1, 13)
        xrl = sem("x_again")

        def cache_load_to(sp, dst, src, g, col, s_):
            x = src.rearrange("s (t q) c -> q (s t) c", q=P)[:, 8 * g:8 * g + 8, col:col + P]
            sp.dma_start(dst, x).then_inc(s_, 16)

        def row_unit(sp, s, n, w, row, half_):
            settle(sp)
            sp.wait_ge(cut_lo[s % 2], n)
            sp.dma_start(raw[s % 2][:].rearrange("p (k c) -> p k c", k=2),
                         w[bass.ds(row, 2 * P), half_ * 512:(half_ + 1) * 512]
                         .rearrange("(k p) c -> p k c", p=P)).then_inc(landed[s % 2], 16)

        block = ctx.enter_context(nc.Block())

        @block.sync
        def _(sp):
            def load_gain(src, n):
                sp.dma_start(gain[:, 0:n], src.rearrange("(a n) -> a n", a=1).broadcast_to([P, n]))\
                  .then_inc(ld("gain"), 16)

            def feature_unit(s, n, w, col):
                if not isinstance(n, int) or n > 0:
                    settle(sp)
                    sp.wait_ge(cut_lo[s % 2], n)
                sp.dma_start(raw[s % 2][:].rearrange("p (k c) -> p k c", k=KB),
                             w.rearrange("(k p) c -> p k c", p=P)[:, :, bass.ds(col, P)]).then_inc(landed[s % 2], 16)

            def column_unit(s, n, w, kb, half_):
                sp.wait_ge(cut_lo[s % 2], n)
                sp.dma_start(raw[s % 2][:].rearrange("p (k c) -> p k c", k=2),
                             w[bass.ds(kb * P, 2 * P), half_ * 512:(half_ + 1) * 512]
                             .rearrange("(k p) c -> p k c", p=P)).then_inc(landed[s % 2], 16)

            sp.dma_start(cst[:], a["cst"]).then_inc(ld("cst"), 16)
            sp.dma_start(c_q[:, 0, 0:(len(LEVELS) + 1) * P], a["lvl"].rearrange("p n c -> p (n c)")).then_inc(ld("cst"), 16)
            for t in range(NT):
                src = a["x_prompt"][t * P:(t + 1) * P, :] if t < SMP else a["x_sample"]
                sp.dma_start(X[:, t, :], src).then_inc(xl[t], 16)
                if t == 0:
                    load_gain(a["norm_mix"], D)
            for s in range(3):
                feature_unit(s, unit_sb(0, s)[1], a["w_in"], s * SBW)
            for s in range(2):
                feature_unit(s, unit_sb(1, s)[1], a["w_in"], P + s * SBW)

            def pair_caches(p, col, g):
                settle(sp)
                if g == 0:
                    sp.wait_ge(sb_kT, p + 1)
                else:
                    sp.wait_ge(sb_tc, p * NC + of_K[0][-1] + 1)
                cache_load(s_cK, a["cache_sb_k"], g, col, sb_cK)
                if g == 1:
                    settle(sp)
                    sp.wait_ge(sb_av, p * U + UA + 1)
                cache_load(s_cV, a["cache_sb_v"], g, col, sb_cV)

            def pair_stores(p, col):
                for buf, done, dp, ds_ in ((s_k, sb_k, o["kp"], o["ks"]), (s_v, sb_v, o["vp"], o["vs"])):
                    settle(sp)
                    sp.wait_ge(done, p * 3 + 3)
                    sp.dma_start(dp.rearrange("(t p) c -> p t c", p=P)[:, :, bass.ds(col, P)],
                                 buf[:, 0:SMP, :]).then_inc(sb_st, 16)
                    sp.dma_start(ds_[:, bass.ds(col, P)], buf[:, SMP, :]).then_inc(sb_st, 16)

            def pair_turn(p, last_of_turn, first_after):
                col = sp.snap(p * P) if not isinstance(p, int) else p * P
                last_of_turn()
                pair_caches(p, col, 0)
                pair_stores(p, col)
                first_after()
                pair_caches(p, col, 1)
                settle(sp)
                sp.wait_ge(sb_x, p * 3 + 3)
                sp.dma_start(mix_t[:, :, bass.ds(col, P)], s_out[:]).then_inc(sb_st, 16)

            def cache_load(buf, src, g, col, s_):
                x = src.rearrange("s (t q) c -> q (s t) c", q=P)[:, 8 * g:8 * g + 8, :]
                sp.dma_start(buf[:], x[:, :, bass.ds(col, P)]).then_inc(s_, 16)

            sp.wait_ge(bar, ENGINES * B_MIX)
            with sp.Fori(0, PAIRS - 2) as p:
                c2 = sp.snap(p * P + P + 2 * SBW)
                cols = [sp.snap(p * P + 2 * P + s * SBW) for s in range(2)]

                def first_after():
                    for s in range(2):
                        feature_unit(s, unit_sb(p + 2, s)[1], a["w_in"], cols[s])

                pair_turn(p, lambda: feature_unit(2, unit_sb(p + 1, 2)[1], a["w_in"], c2), first_after)
            hg_unit = lambda h, s: feature_unit(s, unit(h, s)[1], a["w_in"], 3 * SBW + s * HGW + h * P)
            q = PAIRS - 1
            pair_turn(q - 1, lambda: feature_unit(2, unit_sb(q, 2)[1], a["w_in"], q * P + 2 * SBW),
                      lambda: [hg_unit(0, s) for s in range(2)])
            pair_turn(q, lambda: [hg_unit(0, s) for s in (2, 3)], lambda: [hg_unit(1, s) for s in range(3)])
            sp.wait_ge(bar, ENGINES * B_SB)
            sp.dma_start(g_keep[:], a["keep"]).then_inc(ld("keep"), 16)
            sp.dma_start(g_gain[:], a["hg_gain"].rearrange("(a n) -> a n", a=1).broadcast_to([P, HGW]))\
              .then_inc(ld("keep"), 16)

            def head_io(h):
                settle(sp)
                sp.wait_ge(G["q"], h + 1)
                sp.dma_start(g_S0[:], a["state"][:, bass.ds(h, 1), :, :].rearrange("s a k v -> k (s a) v"))\
                  .then_inc(G["s0"], 16)

            def head_out(h):
                settle(sp)
                sp.wait_ge(G["s"], h * SMP + SMP)
                sp.dma_start(o["sp"][bass.ds(h, 1)].rearrange("a k v -> k (a v)"), g_S[:, SMP - 1, :])\
                  .then_inc(G["st"], 16)
                settle(sp)
                sp.wait_ge(G["sout"], h + 1)
                sp.dma_start(o["ss"][:, bass.ds(h, 1), :, :].rearrange("s a k v -> k (s a) v"), g_S0[:])\
                  .then_inc(G["st"], 16)
                settle(sp)
                sp.wait_ge(G["x"], h + 1)
                sp.dma_start(mix_t[:, :, bass.ds(h * P + SBW, P)], g_out[:]).then_inc(G["st"], 16)

            def head_turn(h, last_of_turn, first_after):
                last_of_turn()
                head_io(h)
                first_after()
                head_out(h)

            with sp.Fori(0, HG_HEADS - 2) as h:
                c3 = sp.snap(h * P + P + 3 * SBW + 3 * HGW)
                cols = [sp.snap(h * P + 2 * P + 3 * SBW + s * HGW) for s in range(3)]

                def first_after():
                    for s in range(3):
                        feature_unit(s, unit(h + 2, s)[1], a["w_in"], cols[s])

                head_turn(h, lambda: feature_unit(3, unit(h + 1, 3)[1], a["w_in"], c3), first_after)
            q = HG_HEADS - 1
            head_turn(q - 1, lambda: hg_unit(q, 3),
                      lambda: [column_unit(s, unit(R_OUT, s)[1], a["w_out"], 2 * s, 0) for s in range(3)])
            head_turn(q, lambda: column_unit(3, unit(R_OUT, 3)[1], a["w_out"], 6, 0), lambda: None)
            sp.wait_ge(bar, ENGINES * B_HG)
            load_gain(a["sb_gain"], SBW)
            sp.wait_ge(sb_st, 80 * PAIRS)
            sp.wait_ge(G["st"], 48 * HG_HEADS)
            for t in range(NT):
                sp.dma_start(X[:, t, :], mix[t * P:(t + 1) * P, :]).then_inc(xl[t], 16)
            for t in range(NT):
                sp.wait_ge(N["tr"], 2 * (n_sb.base + t + 1))
                src = a["x_prompt"][t * P:(t + 1) * P, :] if t < SMP else a["x_sample"]
                sp.dma_start(X[:, t, :], src).then_inc(xrl, 16)
            sp.wait_ge(bar, ENGINES * B_MN)
            load_gain(a["norm_mem_kv"], D)
            for t in range(2):
                sp.dma_start(c_q[:, t, 0:D], a["mem"][t * P:(t + 1) * P, :]).then_inc(ml[t], 16)
            for s in range(4):
                column_unit(s, unit(R_OUT + 1, s)[1], a["w_out"], 2 * s, 1)
            for s in range(4):
                feature_unit(s, unit(R_MEM, s)[1], a["w_mk"], s * P)
            for s in range(4):
                feature_unit(s, unit(R_MEM + 1, s)[1], a["w_mv"], s * P)
            for s in range(4):
                feature_unit(s, unit(R_MQ, s)[1], a["w_mq"], s * P)
            sp.wait_ge(m_tev, 4)
            sp.dma_start(o["mk"].rearrange("(t p) c -> p t c", p=P), xn[:, 0, :].rearrange("p (t c) -> p t c", t=2))\
              .then_inc(m_st, 16)
            sp.wait_ge(m_tev, 8)
            sp.dma_start(o["mv"].rearrange("(t p) c -> p t c", p=P), c_v[:]).then_inc(m_st, 16)
            sp.wait_ge(m_st, 32)
            sp.wait_ge(bar, ENGINES * B_MEM)
            load_gain(a["norm_mem_q"], D)
            for s in range(4):
                column_unit(s, unit(R_MO, s)[1], a["w_mo"], 2 * (s % 2), s // 2)
            sp.wait_ge(bar, ENGINES * B_MQN)
            for hd in range(MEM_HEADS):
                for g in range(2):
                    n = 2 * hd + g
                    if n:
                        sp.wait_ge(CN["kt"], 2 * n)
                    cache_load_to(sp, xn[:, 0, :].rearrange("p (b c) -> p b c", c=P), a["cache_mem_k"], g, hd * P,
                                  CN["ldK"])
                    if hd:
                        sp.wait_ge(CN["av"], hd * UH)
                    dst = xn[:, 1, :].rearrange("p (b c) -> p b c", c=P) if g == 0 else c_V1[:]
                    cache_load_to(sp, dst, a["cache_mem_v"], g, hd * P, CN["ldV"])
            for s in range(4):
                feature_unit(s, unit(ff_round(0, 0), s)[1], a["w_ffn1"], s * P)
            sp.wait_ge(bar, ENGINES * B_MO)
            load_gain(a["norm_ffn"], D)
            with sp.Fori(0, FG - 1) as g:
                cols = [sp.snap(g * (FB * P) + FB * P + s * P) for s in range(4)]
                kbs = [sp.snap(g * (FB * P) + (s % 2) * 2 * P) for s in range(4)]
                for s in range(4):
                    row_unit(sp, s, unit(ff_round(g, 1), s)[1], a["w_ffn2"], kbs[s], s // 2)
                for s in range(4):
                    feature_unit(s, unit(ff_round(g, 2), s)[1], a["w_ffn1"], cols[s])
            for s in range(4):
                row_unit(sp, s, unit(ff_round(FG - 1, 1), s)[1], a["w_ffn2"],
                         (FG - 1) * FB * P + (s % 2) * 2 * P, s // 2)
            sp.wait_ge(bar, ENGINES * B_FF)
            load_gain(a["norm_final"], D)
            for t in range(NT):
                sp.wait_ge(N["xn"], n_fin.base + t + 1)
                dst = o["yp"][t * P:(t + 1) * P, :] if t < SMP else o["ys"]
                sp.dma_start(dst, xn[:, t % 2, :]).then_inc(N["out"], 16)
                sp.wait_ge(N["out"], 16 * (t + 1))

        @block.gpsimd
        def _(pool):
            pool.memset(half[:], -0.5).then_inc(ld("half"), 1)
            pool.wait_ge(ld("half"), 1)
            norm_pool(pool, n_mix)
            barrier(pool, B_MIX)
            barrier(pool, B_SB)
            hg_pool(pool)
            barrier(pool, B_HG)
            norm_pool(pool, n_sb)
            barrier(pool, B_MN)
            barrier(pool, B_WO)
            norm_pool(pool, n_mem)
            barrier(pool, B_MEM)
            norm_pool(pool, n_mq)
            barrier(pool, B_MQN)
            barrier(pool, B_CR)
            barrier(pool, B_MO)
            norm_pool(pool, n_ff)
            barrier(pool, B_FN)
            barrier(pool, B_FF)
            norm_pool(pool, n_fin)

        @block.tensor
        def _(pe):
            for s in range(SLOTS):
                pe.sem_inc(slot_free[s], 1)
            pe.wait_ge(ld("cst"), 32)
            norm_pe(pe, n_mix)
            barrier(pe, B_MIX)
            sb_pe(pe)
            barrier(pe, B_SB)
            hg_pe(pe)
            barrier(pe, B_HG)
            norm_pe(pe, n_sb)
            barrier(pe, B_MN)
            out_pe(pe, wo_s, R_OUT, h_hi, h_lo, KB, 4)
            barrier(pe, B_WO)
            norm_pe(pe, n_mem)
            pe.wait_ge(N["lo"], 2 * (n_mem.base + 2))
            mem_pe(pe)
            barrier(pe, B_MEM)
            norm_pe(pe, n_mq)
            barrier(pe, B_MQN)
            mq_pe(pe)
            cross_pe(pe)
            barrier(pe, B_CR)
            out_pe(pe, mo_s, R_MO, h_hi, h_lo, 4, 2)
            barrier(pe, B_MO)
            norm_pe(pe, n_ff)
            barrier(pe, B_FN)
            ff_pe(pe)
            barrier(pe, B_FF)

        @block.scalar
        def _(act):
            act.preload_act_table_set("natural_log_exp_and_others")
            norm_act(act, n_mix)
            for s in range(3):
                cut_hi_unit(act, unit_sb(0, s), s)
            barrier(act, B_MIX)
            sb_act(act)
            barrier(act, B_SB)
            hg_act(act)
            barrier(act, B_HG)
            norm_act(act, n_sb)
            barrier(act, B_MN)
            for s in range(4):
                cut_hi_unit(act, unit(R_OUT + 1, s), s)
            for s in range(4):
                cut_hi_unit(act, unit(R_MEM, s), s)
            barrier(act, B_WO)
            norm_act(act, n_mem)
            mem_act(act)
            barrier(act, B_MEM)
            act.wait_ge(m_st, 32)
            norm_act(act, n_mq)
            barrier(act, B_MQN)
            mq_act(act)
            cross_act(act)
            barrier(act, B_CR)
            for s in range(4):
                cut_hi_unit(act, unit(ff_round(0, 0), s), s)
            barrier(act, B_MO)
            norm_act(act, n_ff)
            barrier(act, B_FN)
            ff_act(act)
            barrier(act, B_FF)
            norm_act(act, n_fin)

        @block.vector
        def _(dve):
            dve.wait_ge(ld("cst"), 32)
            dve.tensor_copy(lvl[:].rearrange("p n c -> p (n c)"), c_q[:, 0, 0:(len(LEVELS) + 1) * P])
            norm_dve(dve, n_mix)
            for s in range(3):
                cut_lo_unit(dve, unit_sb(0, s), s)
            dve.wait_ge(ld("cst"), 32)
            barrier(dve, B_MIX)
            sb_dve(dve)
            barrier(dve, B_SB)
            dve.wait_ge(ld("keep"), 32)
            hg_dve(dve)
            barrier(dve, B_HG)
            norm_dve(dve, n_sb)
            barrier(dve, B_MN)
            dve.wait_ge(xrl, 16 * NT)

            def between(half_):
                for s in range(4):
                    cut_lo_unit(dve, unit(R_OUT + 1 + half_, s), s)

            out_dve(dve, wo_s, R_OUT, 4, between=between)
            barrier(dve, B_WO)
            norm_dve(dve, n_mem)
            mem_dve(dve)
            barrier(dve, B_MEM)
            norm_dve(dve, n_mq)
            barrier(dve, B_MQN)
            mq_dve(dve)
            cross_dve(dve)
            barrier(dve, B_CR)

            def between_mo(half_):
                for s in (2 * half_, 2 * half_ + 1):
                    cut_lo_unit(dve, unit(ff_round(0, 0), s), s)

            out_dve(dve, mo_s, R_MO, 2, between=between_mo)
            barrier(dve, B_MO)
            norm_dve(dve, n_ff)
            barrier(dve, B_FN)
            ff_dve(dve)
            barrier(dve, B_FF)
            norm_dve(dve, n_fin)


_INS = {
    "x_prompt": (SEQ, D), "x_sample": (NS * NQ, D), "mem": (NMEM, D),
    "cache_sb_k": (NS, PAST, SBW), "cache_sb_v": (NS, PAST, SBW), "state": (NS, HG_HEADS, P, P),
    "cache_mem_k": (NS, NMEM, MEMW), "cache_mem_v": (NS, NMEM, MEMW),
    "norm_mix": (D,), "w_in": (D, 3 * SBW + 4 * HGW), "sb_gain": (SBW,), "hg_gain": (HGW,),
    "w_out": (SBW + HGW, D), "norm_mem_q": (D,), "norm_mem_kv": (D,), "w_mq": (D, MEMW), "w_mk": (D, MEMW),
    "w_mv": (D, MEMW), "w_mo": (MEMW, D), "norm_ffn": (D,), "w_ffn1": (D, DFF), "w_ffn2": (DFF, D),
    "norm_final": (D,),
}
_FROM = {"mem": "mem_prompt", "state": "state_hgrn"}
_OUTS = [
    ("yp", (SEQ, D), (1, SEQ, D)), ("ys", (NS * NQ, D), (NS, NQ, D)),
    ("kp", (SEQ, SBW), (1, 1, SEQ, 8, HD)), ("vp", (SEQ, SBW), (1, 1, SEQ, 8, HD)),
    ("sp", (HG_HEADS, P, P), (1, 1, HG_HEADS, P, P)),
    ("mk", (NMEM, MEMW), (1, 1, NMEM, MEM_HEADS, P)), ("mv", (NMEM, MEMW), (1, 1, NMEM, MEM_HEADS, P)),
    ("ks", (NS * NQ, SBW), (1, NS, NQ, 8, HD)), ("vs", (NS * NQ, SBW), (1, NS, NQ, 8, HD)),
    ("ss", (NS, HG_HEADS, P, P), (1, NS, HG_HEADS, P, P)),
]


def kernel(**inputs):
    import numpy as np
    import concourse.bacc as bacc
    from concourse.bass_utils import run_bass_kernel_spmd

    nc = bacc.Bacc("TRN2", target_bir_lowering=False, num_devices=1)
    cst, lvl, keep = shape_constants()
    arrays = {"cst": cst, "lvl": lvl, "keep": keep}
    for name, shape in _INS.items():
        arrays[name] = np.ascontiguousarray(inputs[_FROM.get(name, name)]).reshape(shape)
    a = {name: nc.dram_tensor(name, x.shape, mybir.dt.from_np(x.dtype), kind="ExternalInput").ap()
         for name, x in arrays.items()}
    o = {name: nc.dram_tensor("out_" + name, shape, F32, kind="ExternalOutput").ap() for name, shape, _ in _OUTS}
    build(nc, a, o)
    r = run_bass_kernel_spmd(nc, [arrays], core_ids=[0])
    return tuple(r.results[0]["out_" + name].reshape(shape) for name, _, shape in _OUTS)
```
